# Optimizing a Trainium2 kernel written in Bass

```python
import jax
import jax.numpy as jnp
from jax import lax
import numpy as np

D_MODEL = 1024
BATCH = 1
SEQ = 1024
DEPTH = 1

GRID_W = 64
CTX_LEN = 256
N_MIXERS = 2
N_LAYERS_A = (DEPTH + N_MIXERS - 1) // N_MIXERS
N_LAYERS_B = DEPTH // N_MIXERS
N_MOD = 6
EPS = 1e-6
DIRECTIONS = (False, True)

D_RNN = 1280
RG_BLOCKS = 10
RG_BLOCK = D_RNN // RG_BLOCKS
RG_C = 8.0
CONV_W = 4
CONV_LEFT = 2

HG_HEADS = 8
HG_DK = 128
HG_WIDTH = HG_HEADS * HG_DK
HG_CHUNK = 64
HG_GROUPS = 5

N_EXPERTS = 16
CAPACITY_FACTOR = 2
EXPERT_FF = 2048

kernel_name = 'hybrid_rglru_hgrn2_ecmoe_dit'

def rms_norm(x, g):
    xf = x.astype(jnp.float32)
    y = xf * lax.rsqrt(jnp.mean(xf * xf, axis=-1, keepdims=True) + EPS)
    return (y * g.astype(jnp.float32)).astype(x.dtype)

def modulate(x, shift, scale):
    return x * (1.0 + scale) + shift

def centred_dwconv(u, w, b):
    length = u.shape[-2]
    pad = [(0, 0)] * (u.ndim - 2) + [(CONV_LEFT, CONV_W - 1 - CONV_LEFT), (0, 0)]
    up = jnp.pad(u, pad)
    return b + sum(w[j] * up[..., j:j + length, :] for j in range(CONV_W))

def _scan_combine(left, right):
    a_l, h_l = left
    a_r, h_r = right
    return a_l * a_r, a_r * h_l + h_r

def diag_scan(a, b, h0, reverse):
    first = -1 if reverse else 0
    b = b.at[:, first].add(a[:, first] * h0)
    _, h = lax.associative_scan(_scan_combine, (a, b), reverse=reverse, axis=1)
    return h

def diag_final_state(log_a, b, reverse):
    if reverse:
        log_a, b = jnp.flip(log_a, 1), jnp.flip(b, 1)
    cum = jnp.cumsum(log_a, axis=1)
    return jnp.sum(jnp.exp(cum[:, -1:] - cum) * b, axis=1)

def rglru_coeffs(u, w_a, b_a, w_x, b_x, lam):
    bsz, length, _ = u.shape
    ub = u.reshape(bsz, length, RG_BLOCKS, RG_BLOCK)
    r = jax.nn.sigmoid(jnp.einsum('blnc,ncd->blnd', ub, w_a).reshape(bsz, length, D_RNN) + b_a)
    i = jax.nn.sigmoid(jnp.einsum('blnc,ncd->blnd', ub, w_x).reshape(bsz, length, D_RNN) + b_x)
    log_a = -RG_C * r * jax.nn.softplus(-lam)
    b = jnp.sqrt(-jnp.expm1(2.0 * log_a)) * (i * u)
    return log_a, b

def rglru_mixer(h_ctx, h_lat, rows, w_in, conv_w, conv_b, w_a, b_a, w_x, b_x, lam, w_out, need_ctx_out):
    f32 = jnp.float32
    bsz, seq, _ = h_lat.shape
    z_lat = (h_lat @ w_in).astype(f32)
    g_lat = z_lat[..., :D_RNN]
    u_lat = centred_dwconv(z_lat[..., D_RNN:].reshape(bsz, rows, GRID_W, D_RNN), conv_w, conv_b)
    u_lat = u_lat.reshape(bsz, seq, D_RNN)
    u_ctx = centred_dwconv((h_ctx @ w_in[:, D_RNN:]).astype(f32), conv_w, conv_b)
    h0 = jnp.zeros((bsz, D_RNN), f32)
    y_lat = 0.0
    y_ctx = 0.0
    for d, reverse in enumerate(DIRECTIONS):
        la_c, b_c = rglru_coeffs(u_ctx, w_a[d], b_a[d], w_x[d], b_x[d], lam[d])
        if need_ctx_out:
            hc = diag_scan(jnp.exp(la_c), b_c, h0, reverse)
            y_ctx = y_ctx + hc
            h_end = hc[:, 0] if reverse else hc[:, -1]
        else:
            h_end = diag_final_state(la_c, b_c, reverse)
        la_l, b_l = rglru_coeffs(u_lat, w_a[d], b_a[d], w_x[d], b_x[d], lam[d])
        y_lat = y_lat + diag_scan(jnp.exp(la_l), b_l, h_end, reverse)
    out_lat = (jax.nn.gelu(g_lat) * y_lat).astype(h_lat.dtype) @ w_out
    if not need_ctx_out:
        return None, out_lat
    g_ctx = (h_ctx @ w_in[:, :D_RNN]).astype(f32)
    out_ctx = (jax.nn.gelu(g_ctx) * y_ctx).astype(h_ctx.dtype) @ w_out
    return out_ctx, out_lat

def hgrn2_chunkwise(q, k, v, log_f, s0):
    bsz, length, nh, dk = q.shape
    n = length // HG_CHUNK
    rs = lambda t: t.reshape(bsz, n, HG_CHUNK, nh, t.shape[-1])
    q, k, v, log_f = rs(q), rs(k), rs(v), rs(log_f)
    cum = jnp.cumsum(log_f, axis=2)
    tot = cum[:, :, -1]
    q_in = q * jnp.exp(cum)
    k_in = k * jnp.exp(-cum)
    k_end = k * jnp.exp(tot[:, :, None] - cum)
    tril = jnp.tril(jnp.ones((HG_CHUNK, HG_CHUNK), bool))
    att = jnp.where(tril, jnp.einsum('bnthk,bnshk->bnhts', q_in, k_in), 0.0)
    o = jnp.einsum('bnhts,bnshv->bnthv', att, v)
    ds = jnp.einsum('bnshk,bnshv->bnhkv', k_end, v)

    def step(s, xs):
        dec, d_s = xs
        return dec[..., None] * s + d_s, s

    s_end, s_prev = lax.scan(step, s0, (jnp.moveaxis(jnp.exp(tot), 1, 0), jnp.moveaxis(ds, 1, 0)))
    o = o + jnp.einsum('bnthk,bnhkv->bnthv', q_in, jnp.moveaxis(s_prev, 0, 1))
    return o.reshape(bsz, length, nh, v.shape[-1]), s_end

def hgrn2_dir(q, k, v, log_f, s0, reverse):
    if reverse:
        q, k, v, log_f = jnp.flip(q, 1), jnp.flip(k, 1), jnp.flip(v, 1), jnp.flip(log_f, 1)
    o, s_end = hgrn2_chunkwise(q, k, v, log_f, s0)
    return (jnp.flip(o, 1) if reverse else o), s_end

def hgrn2_final_state(k, v, log_f, reverse):
    if reverse:
        k, v, log_f = jnp.flip(k, 1), jnp.flip(v, 1), jnp.flip(log_f, 1)
    cum = jnp.cumsum(log_f, axis=1)
    return jnp.einsum('blhk,blhv->bhkv', k * jnp.exp(cum[:, -1:] - cum), v)

def hgrn2_mixer(h_ctx, h_lat, w_in, lb, norm_g, w_out, need_ctx_out):
    f32 = jnp.float32
    W = HG_WIDTH
    heads = lambda t: t.reshape(t.shape[0], t.shape[1], HG_HEADS, HG_DK)
    grp = lambda z, off, g: z[..., g * W - off:(g + 1) * W - off]

    def forget(zf, lb_d):
        f = lb_d + (1.0 - lb_d) * jax.nn.sigmoid(zf)
        return heads(jnp.log(f)), heads((1.0 - lb_d) * jax.nn.sigmoid(-zf))

    def readout(o, g, dtype):
        of = o * lax.rsqrt(jnp.mean(o * o, axis=-1, keepdims=True) + EPS) * norm_g.reshape(HG_HEADS, HG_DK)
        of = of.reshape(o.shape[0], o.shape[1], W) * jax.nn.silu(g)
        return of.astype(dtype) @ w_out

    z = (h_lat @ w_in).astype(f32)
    q_l, i_l = heads(jax.nn.silu(grp(z, 0, 0))), heads(grp(z, 0, 1))
    off = 0 if need_ctx_out else W
    zc = (h_ctx @ w_in[:, off:(HG_GROUPS * W if need_ctx_out else 4 * W)]).astype(f32)
    i_c = heads(grp(zc, off, 1))
    bsz = h_lat.shape[0]
    s0 = jnp.zeros((bsz, HG_HEADS, HG_DK, HG_DK), f32)
    if need_ctx_out:
        q_c = heads(jax.nn.silu(grp(zc, off, 0)))
    o_lat = 0.0
    o_ctx = 0.0
    for d, reverse in enumerate(DIRECTIONS):
        lf_c, k_c = forget(grp(zc, off, 2 + d), lb[d])
        if need_ctx_out:
            o_c, s_end = hgrn2_dir(q_c, k_c, i_c, lf_c, s0, reverse)
            o_ctx = o_ctx + o_c
        else:
            s_end = hgrn2_final_state(k_c, i_c, lf_c, reverse)
        lf_l, k_l = forget(grp(z, 0, 2 + d), lb[d])
        o_l, _ = hgrn2_dir(q_l, k_l, i_l, lf_l, s_end, reverse)
        o_lat = o_lat + o_l
    out_lat = readout(o_lat, grp(z, 0, 4), h_lat.dtype)
    if not need_ctx_out:
        return None, out_lat
    return readout(o_ctx, grp(zc, off, 4), h_ctx.dtype), out_lat

def expert_choice_ffn(h, w_router, w_gate, w_up, w_down):
    bsz, n, dm = h.shape
    cap = CAPACITY_FACTOR * n // N_EXPERTS
    aff = jax.nn.softmax((h @ w_router).astype(jnp.float32), axis=-1)
    gate, idx = lax.top_k(jnp.swapaxes(aff, 1, 2), cap)
    xg = jax.vmap(lambda hb, ib: hb[ib])(h, idx)
    hid = jax.nn.silu(jnp.einsum('becd,edf->becf', xg, w_gate)) * jnp.einsum('becd,edf->becf', xg, w_up)
    y = jnp.einsum('becf,efd->becd', hid, w_down) * gate[..., None].astype(h.dtype)
    return jax.vmap(lambda yb, ib: jnp.zeros((n, dm), yb.dtype).at[ib.reshape(-1)].add(yb.reshape(-1, dm)))(y, idx)

def setup_inputs(seed: int = 0) -> dict:
    key = jax.random.key(seed)
    ks = iter(jax.random.split(key, 32))
    nrm = lambda shape, scale: scale * jax.random.normal(next(ks), shape, jnp.float32)
    D = D_MODEL
    a_pow = jax.random.uniform(next(ks), (N_LAYERS_A, 2, D_RNN), jnp.float32, 0.9, 0.999)
    a_base = a_pow ** (1.0 / RG_C)
    a_lambda = jnp.log(a_base) - jnp.log1p(-a_base)
    return {
        'x': nrm((BATCH, SEQ, D), 1.0),
        'c': nrm((BATCH, D), 1.0),
        'ctx': nrm((BATCH, CTX_LEN, D), 1.0),
        'c_ctx': nrm((D,), 1.0),
        'ada_w': nrm((DEPTH, D, N_MOD * D), 0.5 * D ** -0.5),
        'ada_b': nrm((DEPTH, N_MOD * D), 0.01),
        'norm_mix_g': 1.0 + nrm((DEPTH, D), 0.02),
        'norm_ffn_g': 1.0 + nrm((DEPTH, D), 0.02),
        'final_g': 1.0 + nrm((D,), 0.02),
        'a_w_in': nrm((N_LAYERS_A, D, 2 * D_RNN), D ** -0.5),
        'a_conv_w': nrm((N_LAYERS_A, CONV_W, D_RNN), CONV_W ** -0.5),
        'a_conv_b': nrm((N_LAYERS_A, D_RNN), 0.01),
        'a_gate_wa': nrm((N_LAYERS_A, 2, RG_BLOCKS, RG_BLOCK, RG_BLOCK), RG_BLOCK ** -0.5),
        'a_gate_ba': nrm((N_LAYERS_A, 2, D_RNN), 0.01),
        'a_gate_wx': nrm((N_LAYERS_A, 2, RG_BLOCKS, RG_BLOCK, RG_BLOCK), RG_BLOCK ** -0.5),
        'a_gate_bx': nrm((N_LAYERS_A, 2, D_RNN), 0.01),
        'a_lambda': a_lambda,
        'a_w_out': nrm((N_LAYERS_A, D_RNN, D), D_RNN ** -0.5),
        'b_w_in': nrm((N_LAYERS_B, D, HG_GROUPS * HG_WIDTH), D ** -0.5),
        'b_lb_logits': nrm((2, DEPTH, HG_WIDTH), 0.1),
        'b_norm_g': 1.0 + nrm((N_LAYERS_B, HG_WIDTH), 0.02),
        'b_w_out': nrm((N_LAYERS_B, HG_WIDTH, D), HG_WIDTH ** -0.5),
        'router_w': nrm((DEPTH, D, N_EXPERTS), D ** -0.5),
        'exp_w_gate': nrm((DEPTH, N_EXPERTS, D, EXPERT_FF), D ** -0.5),
        'exp_w_up': nrm((DEPTH, N_EXPERTS, D, EXPERT_FF), D ** -0.5),
        'exp_w_down': nrm((DEPTH, N_EXPERTS, EXPERT_FF, D), EXPERT_FF ** -0.5),
    }

def reference(x, c, ctx, c_ctx, ada_w, ada_b, norm_mix_g, norm_ffn_g, final_g,
              a_w_in, a_conv_w, a_conv_b, a_gate_wa, a_gate_ba, a_gate_wx, a_gate_bx, a_lambda, a_w_out,
              b_w_in, b_lb_logits, b_norm_g, b_w_out,
              router_w, exp_w_gate, exp_w_up, exp_w_down):
    rows = x.shape[1] // GRID_W
    p = jax.nn.softmax(b_lb_logits.astype(jnp.float32), axis=1)
    lower_bounds = jnp.cumsum(p, axis=1) - p
    silu_c = jax.nn.silu(c)
    silu_cc = jax.nn.silu(c_ctx)
    for l in range(DEPTH):
        last = l == DEPTH - 1
        j = l // N_MIXERS
        mod = (silu_c @ ada_w[l] + ada_b[l]).reshape(x.shape[0], N_MOD, 1, D_MODEL)
        n_cm = 2 if last else N_MOD
        mod_c = (silu_cc @ ada_w[l, :, :n_cm * D_MODEL] + ada_b[l, :n_cm * D_MODEL]).reshape(n_cm, D_MODEL)
        h_lat = modulate(rms_norm(x, norm_mix_g[l]), mod[:, 0], mod[:, 1])
        h_ctx = modulate(rms_norm(ctx, norm_mix_g[l]), mod_c[0], mod_c[1])
        if l % N_MIXERS == 0:
            y_ctx, y_lat = rglru_mixer(h_ctx, h_lat, rows, a_w_in[j], a_conv_w[j], a_conv_b[j],
                                       a_gate_wa[j], a_gate_ba[j], a_gate_wx[j], a_gate_bx[j],
                                       a_lambda[j], a_w_out[j], not last)
        else:
            y_ctx, y_lat = hgrn2_mixer(h_ctx, h_lat, b_w_in[j], lower_bounds[:, l], b_norm_g[j],
                                       b_w_out[j], not last)
        x = x + mod[:, 2] * y_lat
        h = modulate(rms_norm(x, norm_ffn_g[l]), mod[:, 3], mod[:, 4])
        x = x + mod[:, 5] * expert_choice_ffn(h, router_w[l], exp_w_gate[l], exp_w_up[l], exp_w_down[l])
        if not last:
            ctx = ctx + mod_c[2] * y_ctx
            hc = modulate(rms_norm(ctx, norm_ffn_g[l]), mod_c[3], mod_c[4])
            ctx = ctx + mod_c[5] * expert_choice_ffn(hc, router_w[l], exp_w_gate[l], exp_w_up[l], exp_w_down[l])
    return rms_norm(x, final_g)


_drawn_inputs = setup_inputs


def setup_inputs(seed=0):
    import zlib

    import numpy as np

    out = dict(_drawn_inputs(seed))
    spreads = {}
    factors = {'norm_mix_g': 4.244,
     'norm_ffn_g': 8.0,
     'final_g': 2.927,
     'a_conv_b': 2.885,
     'a_gate_ba': 8.0,
     'a_gate_bx': 8.0}
    for name, (base, spread) in spreads.items():
        noise = np.random.default_rng([zlib.crc32(name.encode()), seed]).standard_normal(out[name].shape)
        drawn = base * np.exp(spread * noise) if base else spread * noise
        out[name] = jnp.asarray(drawn.astype(out[name].dtype))
    for name, factor in factors.items():
        out[name] = (out[name] * factor).astype(out[name].dtype)
    return out
```

```python
from contextlib import ExitStack

import concourse.bass as bass
from concourse import mybir

F32 = mybir.dt.float32
F32R = mybir.dt.float32r
I32 = mybir.dt.int32
U32 = mybir.dt.uint32
ALU = mybir.AluOpType
ACT = mybir.ActivationFunctionType
AX = mybir.AxisListType
KB = 1024


def program(nc, stack, x, c, ctx, c_ctx, ada_w, ada_b, norm_mix_g, norm_ffn_g, final_g, a_w_in, a_conv_w,
            a_conv_b, a_gate_wa, a_gate_ba, a_gate_wx, a_gate_bx, a_lambda, a_w_out, router_w,
            exp_w_gate, exp_w_up, exp_w_down, out):
    P = 128
    SEQ, D = x.shape[1:]
    CTX = ctx.shape[1]
    KD = D // P
    NT = SEQ // P
    NCT = CTX // P
    LEN = SEQ + CTX
    D_RNN = a_w_out.shape[1]
    NB = D_RNN // P
    GRID_W = 64
    ROWS = SEQ // GRID_W
    TAPS, CENTRE = 4, 2
    E = router_w.shape[2]
    CAP = 2 * SEQ // E
    FF = exp_w_gate.shape[3]
    HALF = 512
    NF = FF // HALF
    EPS = 1e-6
    RG_C = 8.0
    assert CAP == P and KD * LEN == NB * D and NF == 4
    SEGS = [(0, HALF), (HALF, HALF), (SEQ, CTX)]

    base = nc.sbuf_base
    base += -base % 64

    def place(name, shape, dtype, kb):
        return nc.alloc_sbuf_tensor_at(name, shape, dtype, offset=base + int(kb * KB))

    act_h = place("act_h", [P, KD * LEN], F32R, 0)
    act_l = place("act_l", [P, KD * LEN], F32R, 40)
    hT_h = act_h[:].rearrange("p (k t) -> p k t", k=KD)
    hT_l = act_l[:].rearrange("p (k t) -> p k t", k=KD)
    wo_h = act_h[:].rearrange("p (n d) -> p n d", n=NB)
    wo_l = act_l[:].rearrange("p (n d) -> p n d", n=NB)
    win_raw = place("win_raw", [P, KD, 2 * P], F32, 80)
    gate_raw = place("gate_raw", [P, 4, P], F32, 88)
    win_h = [place(f"win_h{s}", [P, KD, 2 * P], F32R, 90 + 20 * s) for s in range(2)]
    win_l = [place(f"win_l{s}", [P, KD, 2 * P], F32R, 98 + 20 * s) for s in range(2)]
    gatew_h = [place(f"gatew_h{s}", [P, 4, P], F32R, 106 + 20 * s) for s in range(2)]
    gatew_l = [place(f"gatew_l{s}", [P, 4, P], F32R, 108 + 20 * s) for s in range(2)]
    ada_buf = place("ada_buf", [P, KD, HALF], F32, 130)
    u = place("u", [P, LEN], F32, 146)
    u_h = place("u_h", [P, LEN], F32R, 151)
    u_l = place("u_l", [P, LEN], F32R, 156)
    r_d = [place("r_fwd", [P, LEN], F32, 161), place("r_bwd", [P, LEN], F32, 171)]
    i_d = [place("i_fwd", [P, LEN], F32, 166), place("i_bwd", [P, LEN], F32, 176)]
    a_d = [place("a_fwd", [P, LEN], F32, 181), place("a_bwd", [P, LEN], F32, 151)]
    t_d = [place("t_fwd", [P, LEN], F32, 186), place("t_bwd", [P, LEN], F32, 156)]
    y_h = place("y_h", [P, SEQ], F32R, 166)
    y_l = place("y_l", [P, SEQ], F32R, 176)
    y = place("y", [P, SEQ], F32, 191)
    xbuf = place("xbuf", [P, NT + NCT, D], F32, 146)
    ada_buf2 = place("ada_buf2", [P, KD, HALF], F32, 110)
    mod_rows = place("mod_rows", [2, 2, HALF], F32, 186)
    junk = place("junk", [P, D], F32, 191)
    hf = place("hf", [P, 2, HALF], F32, 195)
    mod_out = place("mod_out", [1, 2, HALF], F32, 195)
    mod_bias = place("mod_bias", [1, 1, HALF], F32, 199)
    SM = 203
    ident = place("ident", [P, P], F32, SM)
    vec1 = place("vec1", [P, 120], F32, SM + 0.5)
    taps = place("taps", [P, TAPS * NB], F32, SM + 1)
    silu_c = place("silu_c", [P, 2, KD], F32, SM + 1.1875)
    rate = place("rate", [P, 2, 20], F32, SM + 1.25)
    mod_col = place("mod_col", [P, 2, 16], F32, SM + 1.4375)
    scale1 = place("scale1", [P, 2, KD], F32, SM + 1.5625)
    scale2 = place("scale2", [P, KD], F32, SM + 1.625)
    shift2 = place("shift2", [P, KD], F32, SM + 1.65625)
    eps = place("eps", [P, 1], F32, SM + 1.6875)
    stat = place("stat", [P, 2, 12], F32, SM + 1.71875)
    tok_id = place("tok_id", [P, E], I32, SM + 1.8125)
    gate_v = place("gate_v", [P, E], F32, SM + 1.875)
    block_col = [place(f"block_col{s}", [P, 13], F32, SM + 2.6875 + s * 0.0625) for s in range(2)]
    id_gather = place("id_gather", [P, 1], I32, SM + 1.9375)
    id_scatter = place("id_scatter", [P, 1], I32, SM + 1.96875)
    soft = place("soft", [P, 8, 20], F32, SM + 2)
    rows1 = place("rows1", [P, P], F32, 199)
    rows2 = place("rows2", [P, P], F32, 199.5)
    yt_h = [place(f"yt_h{s}", [P, NB, P], F32R, 146 + 10 * s) for s in range(2)]
    yt_l = [place(f"yt_l{s}", [P, NB, P], F32R, 151 + 10 * s) for s in range(2)]
    xt = [place(f"xt{s}", [P, D], F32, 166 + 4 * s) for s in range(2)]
    x2 = [place(f"x2_{s}", [P, D], F32, 174 + 4 * s) for s in range(2)]
    xn = [place(f"xn{s}", [P, D], F32, 182 + 4 * s) for s in range(2)]
    h2T = place("h2T", [P, KD, P], F32, 190)
    gate2_row = place("gate2_row", [P, D], F32, 195)
    gate5_row = place("gate5_row", [P, D], F32, 199)
    router = place("router", [P, KD, E], F32, 194)
    rows3 = place("rows3", [2 * KD, P], F32, 194.5)
    aff_row = [place(f"aff_row{s}", [E, SEQ], F32, 166 + 4 * s) for s in range(2)]
    top_val = place("top_val", [E, CAP], F32, 174)
    top_id = place("top_id", [E, CAP], U32, 174.5)
    top_idf = place("top_idf", [E, CAP], F32, 175)
    NS = 6
    part_h = [place(f"part_h{s}", [P, 4 * HALF], F32R, 16 * s) for s in range(NS)]
    part_l = [place(f"part_l{s}", [P, 4 * HALF], F32R, 16 * s + 8) for s in range(NS)]
    raw = [place(f"raw{s}", [P, 4 * HALF], F32, 96 + 8 * s) for s in range(NS)]
    xg = place("xg", [P, D], F32, 146)
    xgT = place("xgT", [P, KD, P], F32, 150)
    xgT_h = place("xgT_h", [P, KD, P], F32R, 154)
    xgT_l = place("xgT_l", [P, KD, P], F32R, 158)
    act_g = [place(f"act_g{s}", [P, HALF], F32, 162 + 2 * s) for s in range(2)]
    hid = [place(f"hid{s}", [P, HALF], F32, 176 + 2 * s) for s in range(2)]
    hidT_h = [place(f"hidT_h{s}", [P, 4, P], F32R, 180 + 4 * s) for s in range(2)]
    hidT_l = [place(f"hidT_l{s}", [P, 4, P], F32R, 182 + 4 * s) for s in range(2)]
    y_out = place("y_out", [P, D], F32, 188)
    fin_in = place("fin_in", [P, NT, D], F32, 0)
    fin_out = place("fin_out", [P, NT, D], F32, 32)
    fin_g = place("fin_g", [P, D], F32, 64)
    fin_junk = place("fin_junk", [P, D], F32, 68)
    assert base + 206 * KB <= nc.sbuf_usable_end

    psum = nc.alloc_psum_tensor("psum", [P, 8, HALF], F32)
    pu = psum[:, 0:3, :].rearrange("p b f -> p (b f)")
    bank = lambda b: psum[:, b, :]

    y_scr = nc.dram_tensor("y_scr", [2, NB, P, SEQ], F32).ap()
    x_scr = nc.dram_tensor("x_scr", [SEQ, D], F32).ap()
    n_scr = nc.dram_tensor("n_scr", [SEQ, D], F32).ap()
    mod_scr = nc.dram_tensor("mod_scr", [4 * D], F32).ap()

    ada_v = ada_w[0].rearrange("(k p) f -> p k f", p=P)
    win_v = a_w_in[0].rearrange("(k p) f -> p k f", p=P)
    wo_v = a_w_out[0].rearrange("(n p) d -> p n d", p=P)
    wa_v = a_gate_wa[0].rearrange("d n c e -> n c d e")
    wx_v = a_gate_wx[0].rearrange("d n c e -> n c d e")
    wg_v = exp_w_gate[0].rearrange("e (k p) f -> e p k f", p=P)
    wu_v = exp_w_up[0].rearrange("e (k p) f -> e p k f", p=P)
    wd_v = exp_w_down[0].rearrange("e (k p) f -> e p k f", p=P)

    names = """small_loaded ident_ready ada_loaded_a ada_loaded_b vec_turned vec_ready
        silu_ready mod_rows_done mod_rows_ready mod_turned mod_col_ready softplus_step squares_done rms_done
        rstd_ready xn_ready x_turned hf_ready hT_h_ready hT_l_ready
        win_loaded win_h_ready win_l_ready u_done g_done gate_done conv_init conv_done u_h_ready
        u_l_ready gelu_done sig_done a_done t_done v_done q_done w_done s_done b_done scan_ctx
        scan_done y_sum y_done y_h_ready y_l_ready y_stored ada_chunk_loaded ada_done
        ada_out mod_stored wo_loaded wo_h_ready wo_l_ready late_loaded rows3_turned mod2_step
        yt_loaded_a yt_loaded_b xt_loaded_a xt_loaded_b proj_done gated_done x2_ready sq2_done
        rms2_done rstd2_ready xn2_ready xn_turned h2T_ready logits_done
        soft_step exp_done aff_turned aff_row_ready top_step top_turned chosen_ready
        id_ready first_id_ready gathered xg_turned xgT_ready xgT_h_ready xgT_l_ready part_h_ready part_l_ready
        chunk_used silu_done hid_ready hid_turned hidT_h_ready hidT_l_ready
        y_ready id2_ready scattered fin_g_loaded fin_sq fin_rms fin_rstd
        fin_ready fin_stored""".split()
    raw_loaded = [stack.enter_context(nc.semaphore(f"raw_loaded{i}")) for i in range(NS)]

    x_loaded = [stack.enter_context(nc.semaphore(f"x_loaded{t}")) for t in range(NT + NCT)]
    fin_loaded = [stack.enter_context(nc.semaphore(f"fin_loaded{t}")) for t in range(NT)]
    x2_stored = [stack.enter_context(nc.semaphore(f"x2_stored{i}")) for i in range(2)]
    n_stored = [stack.enter_context(nc.semaphore(f"n_stored{i}")) for i in range(2)]
    PER_SLOT = 16 * NT // 2

    sem = {n: stack.enter_context(nc.semaphore(n)) for n in names}

    V_ADA, V_NM, V_NF, V_CB, V_BA, V_BX, V_LAM, V_C = 0, 16, 24, 32, 42, 62, 82, 102
    V_END = V_C + 2 * KD
    as_rows = lambda ap, pat: ap.rearrange(pat, q=P)
    small = [
        (rows1, V_ADA, as_rows(ada_b[0, 0:2 * D], "(r q) -> r q"), 2 * KD),
        (rows1, V_NM, as_rows(norm_mix_g[0], "(r q) -> r q"), KD),
        (rows1, V_NF, as_rows(norm_ffn_g[0], "(r q) -> r q"), KD),
        (rows1, V_CB, as_rows(a_conv_b[0], "(r q) -> r q"), NB),
        (rows1, V_BA, as_rows(a_gate_ba[0], "d (r q) -> (d r) q"), 2 * NB),
        (rows1, V_BX, as_rows(a_gate_bx[0], "d (r q) -> (d r) q"), 2 * NB),
        (rows1, V_LAM, as_rows(a_lambda[0], "d (r q) -> (d r) q"), 2 * NB),
        (rows1, V_C, as_rows(c[0], "(r q) -> r q"), KD),
        (rows1, V_C + KD, as_rows(c_ctx, "(r q) -> r q"), KD),
        (rows2, 0, as_rows(a_conv_w[0], "j (r q) -> (j r) q"), TAPS * NB),
    ]
    N_ADA1 = 2 * D // HALF
    N_ADA2 = 4 * D // HALF
    ada1 = [ada_buf, ada_buf2]
    ada_sem = [sem["ada_loaded_a"], sem["ada_loaded_b"]]
    seg_tiles = [range(0, 4), range(4, 8), range(NT, NT + NCT)]
    groups = [(g, k) for g in range(3) for k in range(KD)]

    order = [("d", 3, 0), ("d", 3, 1)]
    for f in range(NF):
        order += [("g", f, 0), ("g", f, 1), ("u", f, 0), ("u", f, 1)]
        if f:
            order += [("d", f - 1, 0), ("d", f - 1, 1)]
    CH = len(order)
    assert CH % NS == 0
    at = {key: i for i, key in enumerate(order)}
    used = lambda e, key: e * CH + at[key] - 1
    gate_at = lambda e, f: used(e, ("g", f, 1))
    up_at = lambda e, f: used(e, ("u", f, 1))
    down_at = lambda e, f: used(e + 1 if f == NF - 1 else e, ("d", f, 1))
    two_before = lambda e, f: (e, f - 2) if f >= 2 else (e - 1, f - 2 + NF)

    def wait_past(eng, signal, value):
        if not (isinstance(value, int) and value <= 0):
            eng.wait_ge(signal, value)

    with nc.Block() as block:

        @block.sync
        def _(sp):
            for dst, row, src, n in small:
                sp.dma_start(dst[row:row + n, :], src).then_inc(sem["small_loaded"], 16)

            def load_ada1(i):
                if i >= 2:
                    sp.wait_ge(sem["mod_rows_done"], i - 1)
                sp.dma_start(ada1[i % 2][:], ada_v[:, :, i * HALF:(i + 1) * HALF]).then_inc(ada_sem[i % 2], 16)

            def load_x(t):
                src = x[0, t * P:(t + 1) * P, :] if t < NT else ctx[0, (t - NT) * P:(t - NT + 1) * P, :]
                sp.dma_start(xbuf[:, t, :], src).then_inc(x_loaded[t], 16)

            def load_block(n):
                sp.dma_start(win_raw[:, :, 0:P], win_v[:, :, bass.ds(n * P, P)]).then_inc(sem["win_loaded"], 16)
                sp.dma_start(win_raw[:, :, P:2 * P], win_v[:, :, bass.ds(n * P + D_RNN, P)]).then_inc(sem["win_loaded"], 16)
                sp.dma_start(gate_raw[:, 0:2, :], wa_v[bass.ds(n, 1)].rearrange("o c d e -> (o c) d e")).then_inc(sem["win_loaded"], 16)
                sp.dma_start(gate_raw[:, 2:4, :], wx_v[bass.ds(n, 1)].rearrange("o c d e -> (o c) d e")).then_inc(sem["win_loaded"], 16)

            def load_ada2(n):
                sp.wait_ge(sem["ada_out"], n)
                sp.dma_start(ada_buf[:], ada_v[:, :, bass.ds(n * HALF + 2 * D, HALF)]).then_inc(sem["ada_chunk_loaded"], 16)
                sp.dma_start(mod_bias[:, 0, :], ada_b[0:1, bass.ds(n * HALF + 2 * D, HALF)]).then_inc(sem["ada_chunk_loaded"], 16)

            load_ada1(0)
            for t in range(0, 4):
                load_x(t)
            load_ada1(1)
            for t in range(4, NT + NCT):
                load_x(t)
            load_block(0)
            load_ada1(2)
            load_ada1(3)
            sp.wait_ge(sem["mod_rows_done"], N_ADA1)
            sp.wait_ge(sem["vec_ready"], 2)
            load_ada2(0)

            def block_loads(n, ada=True):
                sp.wait_ge(sem["win_h_ready"], n)
                sp.wait_ge(sem["win_l_ready"], n)
                load_block(n)
                if ada:
                    load_ada2(n)

            with sp.Fori(1, N_ADA2) as n:
                block_loads(n)
            for n in range(N_ADA2, NB):
                block_loads(n, ada=False)

            for i in range(NB // 2):
                if i == 0:
                    sp.wait_ge(sem["win_h_ready"], NB)
                    sp.wait_ge(sem["win_l_ready"], NB)
                else:
                    sp.wait_ge(sem["wo_h_ready"], i)
                    sp.wait_ge(sem["wo_l_ready"], i)
                sp.dma_start(win_raw[:].rearrange("p k f -> p (k f)").rearrange("p (n d) -> p n d", n=2),
                             wo_v[:, 2 * i:2 * i + 2, :]).then_inc(sem["wo_loaded"], 16)
            sp.wait_ge(sem["mod_stored"], 16 * N_ADA2)
            sp.wait_ge(sem["y_l_ready"], NB)
            sp.wait_ge(sem["y_h_ready"], NB)
            row_of = lambda ap: ap.rearrange("(o f) -> o f", o=1).broadcast_to((P, D))
            sp.dma_start(gate2_row[:], row_of(mod_scr[0:D])).then_inc(sem["late_loaded"], 16)
            sp.dma_start(gate5_row[:], row_of(mod_scr[3 * D:4 * D])).then_inc(sem["late_loaded"], 16)
            sp.dma_start(rows3[:], mod_scr[D:3 * D].rearrange("(r q) -> r q", q=P)).then_inc(sem["late_loaded"], 16)
            sp.dma_start(router[:], router_w[0].rearrange("(k p) e -> p k e", p=P)).then_inc(sem["late_loaded"], 16)
            sp.wait_ge(sem["y_stored"], 32 * NB)

            def tile_loads(t, slot, j):
                if j is not None:
                    sp.wait_ge(sem["proj_done"], (t - 1) * 2)
                    sp.wait_ge(sem["x2_ready"], t - 1)
                cols = bass.ds(t * P, P)
                yt_loaded = [sem["yt_loaded_a"], sem["yt_loaded_b"]][slot]
                sp.dma_start(yt_h[slot][:].bitcast(F32), y_scr[0].rearrange("n c t -> c n t")[:, :, cols]).then_inc(yt_loaded, 16)
                sp.dma_start(yt_l[slot][:].bitcast(F32), y_scr[1].rearrange("n c t -> c n t")[:, :, cols]).then_inc(yt_loaded, 16)
                sp.dma_start(xt[slot][:], x[0, cols, :]).then_inc([sem["xt_loaded_a"], sem["xt_loaded_b"]][slot], 16)

            def tile_stores(t, slot):
                rows = bass.ds(t * P, P)
                sp.wait_ge(sem["x2_ready"], t + 1)
                sp.dma_start(x_scr[rows, :], x2[slot][:]).then_inc(x2_stored[slot], 16)
                sp.wait_ge(sem["xn2_ready"], t + 1)
                sp.dma_start(n_scr[rows, :], xn[slot][:]).then_inc(n_stored[slot], 16)

            tile_loads(0, 0, None)
            tile_loads(1, 1, None)
            with sp.Fori(0, NT // 2 - 1) as j:
                for slot in range(2):
                    tile_stores(j * 2 + slot, slot)
                    tile_loads(j * 2 + slot + 2, slot, j)

            def load_chunk(e, i, first=False):
                kind, f, half = order[i]
                slot = i % NS
                if kind == "d":
                    e_of = e - 1 if f == NF - 1 else e
                    src = wd_v[bass.ds(e_of, 1), :, 4 * f + 2 * half:4 * f + 2 * half + 2, :]
                    dst = raw[slot][:].rearrange("p (k f) -> p k f", k=2)
                else:
                    src = (wg_v if kind == "g" else wu_v)[bass.ds(e, 1), :, 4 * half:4 * half + 4, f * HALF:(f + 1) * HALF]
                    dst = raw[slot][:].rearrange("p (k f) -> p k f", k=4)
                if not first:
                    sp.wait_ge(sem["part_h_ready"], e * CH + i - NS - 1)
                    sp.wait_ge(sem["part_l_ready"], e * CH + i - NS - 1)
                sp.dma_start(dst, src.rearrange("o p k f -> (o p) k f")).then_inc(raw_loaded[slot], 16)

            sp.wait_ge(sem["wo_h_ready"], NB // 2)
            sp.wait_ge(sem["wo_l_ready"], NB // 2)
            sp.wait_ge(sem["gate_done"], 12 * NB)
            for i in range(2, 2 + NS):
                load_chunk(0, i, first=True)
            for t in range(NT - 2, NT):
                tile_stores(t, t % 2)
            for i in range(2 + NS, CH):
                load_chunk(0, i)
            with sp.Fori(1, E) as e:
                for i in range(CH):
                    load_chunk(e, i)
            for i in range(2):
                load_chunk(E, i)

            sp.wait_ge(sem["chunk_used"], E * CH)
            sp.dma_start(fin_g[:], row_of(final_g)).then_inc(sem["fin_g_loaded"], 16)
            sp.wait_ge(sem["scattered"], 16 * E)
            for t in range(NT):
                sp.dma_start(fin_in[:, t, :], x_scr[t * P:(t + 1) * P, :]).then_inc(fin_loaded[t], 16)
            for t in range(NT):
                sp.wait_ge(sem["fin_ready"], t + 1)
                sp.dma_start(out[0, t * P:(t + 1) * P, :], fin_out[:, t, :]).then_inc(sem["fin_stored"], 16)
            sp.wait_ge(sem["fin_stored"], 16 * NT)
            for i in range(2):
                sp.wait_ge(x2_stored[i], PER_SLOT)
                sp.wait_ge(n_stored[i], PER_SLOT)

        @block.gpsimd
        def _(pool):
            nc.gpsimd.memset(ident[:], 0.0).then_inc(sem["ident_ready"], 1)
            nc.gpsimd.memset(eps[:], EPS)
            pool.wait_ge(sem["ident_ready"], 1)
            nc.gpsimd.affine_select(out=ident[:], in_=ident[:], compare_op=ALU.not_equal, fill=1.0, base=0,
                                    pattern=[[-1, P]], channel_multiplier=1).then_inc(sem["ident_ready"], 1)

            def mixer_block(n):
                for d in range(2):
                    pool.wait_ge(sem["sig_done"], n * 12 + 6 * d + 6)
                    nc.gpsimd.tensor_tensor(i_d[d][:], i_d[d][:], u[:], ALU.mult).then_inc(sem["v_done"], 1)
                for d in range(2):
                    pool.wait_ge(sem["t_done"], n * 2 + d + 1)
                    nc.gpsimd.tensor_tensor(r_d[d][:], a_d[d][:], a_d[d][:], ALU.mult).then_inc(sem["q_done"], 1)
                for part, (buf, ready) in enumerate(((y_h, sem["y_h_ready"]), (y_l, sem["y_l_ready"]))):
                    pool.wait_ge(ready, n + 1)
                    pool.dma_start(y_scr[part, bass.ds(n, 1)].rearrange("o c t -> (o c) t"), buf[:].bitcast(F32)).then_inc(sem["y_stored"], 16)

            def store_mod(n):
                pool.wait_ge(sem["ada_out"], n + 1)
                pool.dma_start(mod_scr[bass.ds(n * HALF, HALF)].rearrange("(o f) -> o f", o=1),
                               mod_out[:, 0, :]).then_inc(sem["mod_stored"], 16)

            with pool.Fori(0, N_ADA2) as n:
                store_mod(n)
                mixer_block(n)
            for n in range(N_ADA2, NB):
                mixer_block(n)

            def gather(e, id_sem, count):
                nc.gpsimd.tensor_copy(id_gather[:], tok_id[:, bass.ds(e, 1)]).then_inc(id_sem, 1)
                pool.wait_ge(sem["ident_ready"], 2)
                pool.wait_ge(id_sem, count)
                nc.gpsimd.indirect_dma_start(xg[:], None, n_scr, bass.IndirectOffsetOnAxis(ap=id_gather[:, 0:1], axis=0)
                                             ).then_inc(sem["gathered"], 16)

            def scatter(e, count):
                wait_past(pool, sem["scattered"], e * 16)
                pool.wait_ge(sem["y_ready"], count * 2)
                nc.gpsimd.tensor_copy(id_scatter[:], tok_id[:, bass.ds(e, 1)]).then_inc(sem["id2_ready"], 1)
                pool.wait_ge(sem["ident_ready"], 2)
                pool.wait_ge(sem["id2_ready"], count)
                nc.gpsimd.indirect_dma_start(x_scr, bass.IndirectOffsetOnAxis(ap=id_scatter[:, 0:1], axis=0), y_out[:],
                                             None, compute_op=ALU.add).then_inc(sem["scattered"], 16)

            pool.wait_ge(sem["chosen_ready"], 2)
            for i in range(2):
                pool.wait_ge(x2_stored[i], PER_SLOT)
                pool.wait_ge(n_stored[i], PER_SLOT)
            gather(0, sem["first_id_ready"], 1)
            pool.wait_ge(sem["gathered"], 16)
            pool.wait_ge(sem["xgT_h_ready"], 1)
            gather(1, sem["id_ready"], 1)
            scatter(0, 1)
            with pool.Fori(1, E - 1) as e:
                pool.wait_ge(sem["gathered"], (e + 1) * 16)
                pool.wait_ge(sem["xgT_h_ready"], e + 1)
                gather(e + 1, sem["id_ready"], e + 1)
                scatter(e, e + 1)
            scatter(E - 1, E)
            pool.wait_ge(sem["scattered"], 16 * E)
            pool.wait_ge(sem["y_stored"], 32 * NB)
            pool.wait_ge(sem["mod_stored"], 16 * N_ADA2)

        @block.scalar
        def _(act):
            def copy(dst, src):
                return nc.scalar.activation(dst, src, ACT.Identity)

            act.wait_ge(sem["vec_ready"], 1)
            nc.scalar.activation(silu_c[:].rearrange("p b k -> p (b k)"), vec1[:, V_C:V_END], ACT.Silu).then_inc(sem["silu_ready"], 1)
            act.wait_ge(sem["softplus_step"], 2)
            nc.scalar.activation(soft[:, 2, :], soft[:, 1, :], ACT.Exp, scale=-1.0).then_inc(sem["exp_done"], 1)
            for t in range(NT + NCT):
                act.wait_ge(x_loaded[t], 16)
                nc.scalar.activation(junk[:], xbuf[:, t, :], ACT.Square, accum_out=stat[:, 0, t:t + 1]).then_inc(sem["squares_done"], 1)
                act.wait_ge(sem["squares_done"], t + 1)
                if t % 4 == 3 or t == NT + NCT - 1:
                    lo = t - t % 4
                    act.wait_ge(sem["ident_ready"], 2)
                    nc.scalar.activation(stat[:, 1, lo:t + 1], stat[:, 0, lo:t + 1], ACT.Sqrt, scale=1.0 / D,
                                         bias=eps[:]).then_inc(sem["rms_done"], 1)
            for n, (g, k) in enumerate(groups):
                lo, w = SEGS[g]
                act.wait_ge(sem["hf_ready"], n + 1)
                copy(hT_h[:, k, lo:lo + w], hf[:, n % 2, 0:w]).then_inc(sem["hT_h_ready"], 1)

            def split_win(n, slot):
                act.wait_ge(sem["win_loaded"], n * 64 + 64)
                wait_past(act, sem["gate_done"], (n - 1) * 12)
                copy(win_h[slot][:], win_raw[:])
                copy(gatew_h[slot][:], gate_raw[:]).then_inc(sem["win_h_ready"], 1)

            act.wait_ge(sem["win_loaded"], 64)
            copy(win_h[0][:], win_raw[:])
            copy(gatew_h[0][:], gate_raw[:]).then_inc(sem["win_h_ready"], 1)

            def mixer_block(n, slot, last=False):
                wait_past(act, sem["v_done"], n * 2)
                wait_past(act, sem["u_l_ready"], n)
                act.wait_ge(sem["u_done"], n + 1)
                nc.scalar.activation(u[:], pu[:, 0:LEN], ACT.Identity, scale=block_col[slot][:, 5 + CENTRE:6 + CENTRE],
                                     bias=block_col[slot][:, 0:1]).then_inc(sem["conv_init"], 1)
                act.wait_ge(sem["conv_done"], (n + 1) * 6)
                wait_past(act, sem["scan_done"], n * 2)
                copy(u_h[:], u[:]).then_inc(sem["u_h_ready"], 1)
                if not last:
                    split_win(n + 1, 1 - slot)
                act.wait_ge(sem["g_done"], n + 1)
                wait_past(act, sem["y_l_ready"], n)
                nc.scalar.activation(y[:], psum[:, 3:5, :].rearrange("p b f -> p (b f)"),
                                     ACT.Gelu_apprx_tanh).then_inc(sem["gelu_done"], 1)
                wait_past(act, sem["y_stored"], n * 32)
                wait_past(act, sem["y_sum"], n)
                for m in range(4):
                    d, is_i = divmod(m, 2)
                    col = block_col[slot][:, 1 + 2 * is_i + d:2 + 2 * is_i + d]
                    for g, (lo, w) in enumerate(SEGS):
                        act.wait_ge(sem["gate_done"], n * 12 + 3 * m + g + 1)
                        nc.scalar.activation((i_d if is_i else r_d)[d][:, lo:lo + w], bank(5 + g)[:, 0:w], ACT.Sigmoid,
                                             bias=col).then_inc(sem["sig_done"], 1)
                for d in range(2):
                    act.wait_ge(sem["sig_done"], n * 12 + 6 * d + 3)
                    nc.scalar.activation(a_d[d][:], r_d[d][:], ACT.Exp, scale=block_col[slot][:, 9 + d:10 + d]).then_inc(sem["a_done"], 1)
                    nc.scalar.activation(t_d[d][:], r_d[d][:], ACT.Tanh, scale=block_col[slot][:, 11 + d:12 + d]).then_inc(sem["t_done"], 1)
                for d in range(2):
                    act.wait_ge(sem["w_done"], n * 2 + d + 1)
                    nc.scalar.activation(t_d[d][:], t_d[d][:], ACT.Sqrt).then_inc(sem["s_done"], 1)
                act.wait_ge(sem["y_done"], n + 1)
                copy(y_h[:], y[:]).then_inc(sem["y_h_ready"], 1)

            mixer_block(0, 0)
            mixer_block(1, 1)
            with act.Fori(1, NB // 2 - 1) as j:
                mixer_block(j * 2, 0)
                mixer_block(j * 2 + 1, 1)
            mixer_block(NB - 2, 0)
            mixer_block(NB - 1, 1, last=True)

            act.wait_ge(sem["g_done"], NB)
            for i in range(NB // 2):
                act.wait_ge(sem["wo_loaded"], 16 * (i + 1))
                copy(act_h[:, 2 * i * D:(2 * i + 2) * D], win_raw[:].rearrange("p k f -> p (k f)")).then_inc(sem["wo_h_ready"], 1)

            def norm2(t, slot, j):
                act.wait_ge(sem["x2_ready"], t + 1)
                if j is not None:
                    act.wait_ge(n_stored[slot], j * 16)
                    act.wait_ge(sem["xn_turned"], t - 1)
                nc.scalar.activation(xn[slot][:], x2[slot][:], ACT.Square, accum_out=stat[:, 0, slot:slot + 1]).then_inc(sem["sq2_done"], 1)
                act.wait_ge(sem["sq2_done"], t + 1)
                nc.scalar.activation(stat[:, 1, slot:slot + 1], stat[:, 0, slot:slot + 1], ACT.Sqrt, scale=1.0 / D,
                                     bias=eps[:]).then_inc(sem["rms2_done"], 1)

            def modulate2(t):
                act.wait_ge(sem["xn_turned"], t + 1)
                wait_past(act, sem["logits_done"], t)
                for k in range(KD):
                    last = nc.scalar.activation(h2T[:, k, :], bank(4 + k // 4)[:, (k % 4) * P:(k % 4 + 1) * P], ACT.Identity,
                                                scale=scale2[:, k:k + 1], bias=shift2[:, k:k + 1])
                last.then_inc(sem["h2T_ready"], 1)

            act.wait_ge(sem["mod2_step"], 2)
            norm2(0, 0, None)
            norm2(1, 1, None)
            modulate2(0)
            with act.Fori(1, NT // 2) as j:
                for slot in range(2):
                    t = j * 2 + slot
                    norm2(t, slot, j)
                    modulate2(t - 1)
            modulate2(NT - 1)

            act.wait_ge(sem["soft_step"], 2)
            nc.scalar.activation(soft[:, 0:NT, 0:E], soft[:, 0:NT, 0:E], ACT.Exp).then_inc(sem["exp_done"], 1)

            def split(e, key):
                i = at[key]
                slot = i % NS
                uses = 0 if slot < 2 else 16
                act.wait_ge(raw_loaded[slot], e * (CH // NS * 16) + (i // NS) * 16 + uses)
                if not (isinstance(e, int) and e == 0 and i < 2 + NS):
                    act.wait_ge(sem["chunk_used"], e * CH + i - NS - 1)
                copy(part_h[slot][:], raw[slot][:]).then_inc(sem["part_h_ready"], 1)

            def hidden(e, f):
                act.wait_ge(sem["chunk_used"], gate_at(e, f))
                if not (isinstance(e, int) and e == 0 and f < 2):
                    act.wait_ge(sem["hid_ready"], e * NF + f - 1)
                nc.scalar.activation(act_g[f % 2][:], bank(2 * (f % 2)), ACT.Silu).then_inc(sem["silu_done"], 1)

            def turn_hidden(e, f):
                act.wait_ge(sem["hid_turned"], e * NF + f + 1)
                if not (isinstance(e, int) and e == 0 and f < 2):
                    act.wait_ge(sem["chunk_used"], down_at(*two_before(e, f)))
                copy(hidT_h[f % 2][:], bank(4 + f % 2)).then_inc(sem["hidT_h_ready"], 1)

            def expert(e, first=False):
                if not first:
                    split(e, ("d", 3, 0))
                    split(e, ("d", 3, 1))
                    turn_hidden(e - 1, 3)
                for k in range(KD):
                    if k % 4 == 0:
                        act.wait_ge(sem["xg_turned"], e * 2 + k // 4 + 1)
                    if k == 0:
                        wait_past(act, sem["xgT_l_ready"], e)
                    last = nc.scalar.activation(xgT[:, k, :], bank(k // 4)[:, (k % 4) * P:(k % 4 + 1) * P],
                                                ACT.Identity, scale=scale2[:, k:k + 1], bias=shift2[:, k:k + 1])
                    if k % 4 == 3:
                        last.then_inc(sem["xgT_ready"], 1)
                act.wait_ge(sem["xgT_ready"], e * 2 + 2)
                if not first:
                    act.wait_ge(sem["chunk_used"], up_at(e - 1, NF - 1))
                copy(xgT_h[:], xgT[:]).then_inc(sem["xgT_h_ready"], 1)
                for f in range(NF):
                    for key in (("g", f, 0), ("g", f, 1), ("u", f, 0), ("u", f, 1)):
                        split(e, key)
                    if f:
                        turn_hidden(e, f - 1)
                    hidden(e, f)
                    if f:
                        split(e, ("d", f - 1, 0))
                        split(e, ("d", f - 1, 1))

            expert(0, first=True)
            with act.Fori(1, E) as e:
                expert(e)
            split(E, ("d", 3, 0))
            split(E, ("d", 3, 1))
            turn_hidden(E - 1, 3)

            act.wait_ge(sem["chunk_used"], E * CH)
            for t in range(NT):
                act.wait_ge(fin_loaded[t], 16)
                nc.scalar.activation(fin_junk[:], fin_in[:, t, :], ACT.Square, accum_out=stat[:, 0, t:t + 1]).then_inc(sem["fin_sq"], 1)
                act.wait_ge(sem["fin_sq"], t + 1)
                nc.scalar.activation(stat[:, 1, t:t + 1], stat[:, 0, t:t + 1], ACT.Sqrt, scale=1.0 / D,
                                     bias=eps[:]).then_inc(sem["fin_rms"], 1)

        @block.vector
        def _(dve):
            v = nc.vector

            dve.wait_ge(sem["vec_turned"], 1)
            v.tensor_copy(vec1[:, 0:V_END], bank(3)[:, 0:V_END]).then_inc(sem["vec_ready"], 1)
            v.tensor_copy(taps[:], bank(3)[:, P:P + TAPS * NB]).then_inc(sem["vec_ready"], 1)
            count = [0]

            def step(ins):
                count[0] += 1
                ins.then_inc(sem["softplus_step"], 1)
                dve.wait_ge(sem["softplus_step"], count[0])

            lam = vec1[:, V_LAM:V_LAM + 2 * NB]
            dve.wait_ge(sem["vec_ready"], 2)
            step(v.tensor_scalar(soft[:, 0, :], lam, -1.0, None, ALU.mult))
            step(v.tensor_tensor(soft[:, 1, :], soft[:, 0, :], lam, ALU.max))
            dve.wait_ge(sem["exp_done"], 1)
            step(v.tensor_scalar(soft[:, 3, :], soft[:, 2, :], 2.0, None, ALU.add))
            step(v.reciprocal(soft[:, 4, :], soft[:, 3, :]))
            step(v.tensor_tensor(soft[:, 3, :], soft[:, 2, :], soft[:, 4, :], ALU.mult))
            step(v.tensor_tensor(soft[:, 4, :], soft[:, 3, :], soft[:, 3, :], ALU.mult))
            step(v.tensor_scalar(soft[:, 5, :], soft[:, 4, :], 2.0 / 17, 2.0 / 15, ALU.mult, ALU.add))
            for m in (13, 11, 9, 7, 5, 3, 1):
                step(v.tensor_tensor(soft[:, 5, :], soft[:, 5, :], soft[:, 4, :], ALU.mult))
                step(v.tensor_scalar(soft[:, 5, :], soft[:, 5, :], 2.0 / m, None, ALU.add))
            step(v.tensor_tensor(soft[:, 5, :], soft[:, 5, :], soft[:, 3, :], ALU.mult))
            step(v.scalar_tensor_tensor(soft[:, 6, :], soft[:, 0, :], 0.0, soft[:, 5, :], ALU.max, ALU.add))
            step(v.tensor_scalar(rate[:, 0, :], soft[:, 6, :], -RG_C, None, ALU.mult))
            step(v.tensor_scalar(rate[:, 1, :], soft[:, 6, :], RG_C, None, ALU.mult))

            def mod_chunk(i):
                dve.wait_ge(sem["mod_rows_done"], i + 1)
                if i >= 2:
                    dve.wait_ge(sem["mod_turned"], i - 1)
                v.tensor_copy(mod_rows[:, i % 2, :], bank(i % 2)[0:2, :]).then_inc(sem["mod_rows_ready"], 1)

            def normed(lo, hi, part):
                dve.wait_ge(sem["rms_done"], part + 1)
                v.reciprocal(stat[:, 0, lo:hi], stat[:, 1, lo:hi]).then_inc(sem["rstd_ready"], 1)
                dve.wait_ge(sem["rstd_ready"], part + 1)
                for t in range(lo, hi):
                    v.tensor_scalar(xbuf[:, t, :], xbuf[:, t, :], stat[:, 0, t:t + 1], None, ALU.mult).then_inc(sem["xn_ready"], 1)

            mod_chunk(0)
            normed(0, 4, 0)
            mod_chunk(1)
            normed(4, 8, 1)
            normed(8, 10, 2)
            mod_chunk(2)
            mod_chunk(3)
            dve.wait_ge(sem["mod_turned"], N_ADA1)
            v.tensor_tensor(mod_col[:].rearrange("p b m -> p m b"), bank(2)[:, 0:32].rearrange("p (m b) -> p m b", b=2),
                            vec1[:, V_ADA:V_ADA + 16].rearrange("p (m o) -> p m o", o=1).broadcast_to((P, 16, 2)),
                            ALU.add).then_inc(sem["mod_col_ready"], 1)
            dve.wait_ge(sem["mod_col_ready"], 1)
            for b in range(2):
                v.scalar_tensor_tensor(scale1[:, b, :], mod_col[:, b, KD:2 * KD], 1.0, vec1[:, V_NM:V_NM + KD],
                                       ALU.add, ALU.mult).then_inc(sem["mod_col_ready"], 1)
            dve.wait_ge(sem["mod_col_ready"], 3)
            dve.wait_ge(sem["vec_ready"], 2)
            def modulate(n):
                g, k = groups[n]
                lo, w = SEGS[g]
                b = 1 if g == 2 else 0
                dve.wait_ge(sem["x_turned"], n + 1)
                if n >= 2:
                    dve.wait_ge(sem["hT_h_ready"], n - 1)
                    dve.wait_ge(sem["hT_l_ready"], n - 1)
                v.tensor_scalar(hf[:, n % 2, 0:w], bank(4 + n % 4)[:, 0:w], scale1[:, b, k:k + 1], mod_col[:, b, k:k + 1],
                                ALU.mult, ALU.add).then_inc(sem["hf_ready"], 1)

            def low_part(n):
                g, k = groups[n]
                lo, w = SEGS[g]
                dve.wait_ge(sem["hT_h_ready"], n + 1)
                v.tensor_tensor(hT_l[:, k, lo:lo + w], hf[:, n % 2, 0:w], hT_h[:, k, lo:lo + w].bitcast(F32),
                                ALU.subtract).then_inc(sem["hT_l_ready"], 1)

            for n in range(len(groups)):
                modulate(n)
                if n:
                    low_part(n - 1)
            low_part(len(groups) - 1)

            def split_win(n, slot):
                dve.wait_ge(sem["win_h_ready"], n + 1)
                for lo, hi, src in ((0, 5, vec1[:, V_CB:V_CB + 5 * NB]), (5, 9, taps[:]), (9, 13, rate[:].rearrange("p s c -> p (s c)"))):
                    v.tensor_scalar(block_col[slot][:, lo:hi].rearrange("p (a o) -> p a o", o=1),
                                    src.rearrange("p (a n) -> p a n", n=NB)[:, :, bass.ds(n, 1)], 1.0, None, ALU.mult)
                v.tensor_tensor(win_l[slot][:], win_raw[:], win_h[slot][:].bitcast(F32), ALU.subtract)
                v.tensor_tensor(gatew_l[slot][:], gate_raw[:], gatew_h[slot][:].bitcast(F32),
                                ALU.subtract).then_inc(sem["win_l_ready"], 1)

            split_win(0, 0)

            def mixer_block(n, slot, ada, last=False):
                lat, con = (u[:, 0:SEQ].rearrange("p (r w) -> p r w", w=GRID_W), u[:, SEQ:LEN])
                z_lat, z_con = (pu[:, 0:SEQ].rearrange("p (r w) -> p r w", w=GRID_W), pu[:, SEQ:LEN])
                dve.wait_ge(sem["conv_init"], n + 1)
                for i, j in enumerate([0, 1, 3]):
                    off = j - CENTRE
                    a, b = max(0, -off), max(0, off)
                    col = block_col[slot][:, 5 + j:6 + j]
                    if i:
                        dve.wait_ge(sem["conv_done"], n * 6 + 2 * i)
                    v.scalar_tensor_tensor(lat[:, :, a:GRID_W - b], z_lat[:, :, b:GRID_W - a], col, lat[:, :, a:GRID_W - b],
                                           ALU.mult, ALU.add).then_inc(sem["conv_done"], 1)
                    v.scalar_tensor_tensor(con[:, a:CTX - b], z_con[:, b:CTX - a], col, con[:, a:CTX - b],
                                           ALU.mult, ALU.add).then_inc(sem["conv_done"], 1)
                dve.wait_ge(sem["u_h_ready"], n + 1)
                v.tensor_tensor(u_l[:], u[:], u_h[:].bitcast(F32), ALU.subtract).then_inc(sem["u_l_ready"], 1)
                if not last:
                    split_win(n + 1, 1 - slot)
                if ada:
                    dve.wait_ge(sem["ada_done"], n + 1)
                    wait_past(dve, sem["mod_stored"], n * 16)
                    v.tensor_tensor(mod_out[:, 0, :], bank(7)[0:1, :], mod_bias[:, 0, :], ALU.add).then_inc(sem["ada_out"], 1)
                for d in range(2):
                    dve.wait_ge(sem["q_done"], n * 2 + d + 1)
                    v.scalar_tensor_tensor(t_d[d][:], r_d[d][:], 1.0, t_d[d][:], ALU.add, ALU.mult).then_inc(sem["w_done"], 1)
                for d in range(2):
                    dve.wait_ge(sem["s_done"], n * 2 + d + 1)
                    v.tensor_tensor(t_d[d][:], t_d[d][:], i_d[d][:], ALU.mult).then_inc(sem["b_done"], 1)
                    dve.wait_ge(sem["b_done"], n * 2 + d + 1)
                    h = r_d[d]
                    flip = (lambda ap: ap[:, ::-1]) if d else (lambda ap: ap)
                    end = h[:, SEQ:SEQ + 1] if d else h[:, LEN - 1:LEN]
                    v.tensor_tensor_scan(flip(h[:, SEQ:LEN]), flip(a_d[d][:, SEQ:LEN]), flip(t_d[d][:, SEQ:LEN]), 0.0,
                                         ALU.mult, ALU.add).then_inc(sem["scan_ctx"], 1)
                    dve.wait_ge(sem["scan_ctx"], n * 2 + d + 1)
                    v.tensor_tensor_scan(flip(h[:, 0:SEQ]), flip(a_d[d][:, 0:SEQ]), flip(t_d[d][:, 0:SEQ]), end,
                                         ALU.mult, ALU.add).then_inc(sem["scan_done"], 1)
                dve.wait_ge(sem["scan_done"], n * 2 + 2)
                v.tensor_tensor(r_d[0][:, 0:SEQ], r_d[0][:, 0:SEQ], r_d[1][:, 0:SEQ], ALU.add).then_inc(sem["y_sum"], 1)
                dve.wait_ge(sem["y_sum"], n + 1)
                dve.wait_ge(sem["gelu_done"], n + 1)
                v.tensor_tensor(y[:], y[:], r_d[0][:, 0:SEQ], ALU.mult).then_inc(sem["y_done"], 1)
                dve.wait_ge(sem["y_h_ready"], n + 1)
                v.tensor_tensor(y_l[:], y[:], y_h[:].bitcast(F32), ALU.subtract).then_inc(sem["y_l_ready"], 1)

            mixer_block(0, 0, True)
            mixer_block(1, 1, True)
            with dve.Fori(1, NB // 2 - 1) as j:
                mixer_block(j * 2, 0, True)
                mixer_block(j * 2 + 1, 1, True)
            mixer_block(NB - 2, 0, False)
            mixer_block(NB - 1, 1, False, last=True)

            for i in range(NB // 2):
                dve.wait_ge(sem["wo_h_ready"], i + 1)
                cols = slice(2 * i * D, (2 * i + 2) * D)
                v.tensor_tensor(act_l[:, cols], win_raw[:].rearrange("p k f -> p (k f)"), act_h[:, cols].bitcast(F32),
                                ALU.subtract).then_inc(sem["wo_l_ready"], 1)

            dve.wait_ge(sem["rows3_turned"], 1)
            v.tensor_copy(shift2[:], bank(7)[:, 0:KD]).then_inc(sem["mod2_step"], 1)
            v.scalar_tensor_tensor(scale2[:], bank(7)[:, KD:2 * KD], 1.0, vec1[:, V_NF:V_NF + KD], ALU.add, ALU.mult).then_inc(sem["mod2_step"], 1)

            def residual(t, slot, j):
                for half in range(2):
                    dve.wait_ge(sem["proj_done"], t * 2 + half + 1)
                    if j is not None:
                        dve.wait_ge(x2_stored[slot], j * 16)
                    cols = slice(half * HALF, (half + 1) * HALF)
                    v.tensor_tensor(x2[slot][:, cols], bank(2 * slot + half), gate2_row[:, cols], ALU.mult).then_inc(sem["gated_done"], 1)
                dve.wait_ge(sem["gated_done"], t * 2 + 2)
                v.tensor_tensor(x2[slot][:], x2[slot][:], xt[slot][:], ALU.add).then_inc(sem["x2_ready"], 1)

            def scale_rows(t, slot):
                dve.wait_ge(sem["rms2_done"], t + 1)
                v.reciprocal(stat[:, 0, slot:slot + 1], stat[:, 1, slot:slot + 1]).then_inc(sem["rstd2_ready"], 1)
                dve.wait_ge(sem["rstd2_ready"], t + 1)
                v.tensor_scalar(xn[slot][:], x2[slot][:], stat[:, 0, slot:slot + 1], None, ALU.mult).then_inc(sem["xn2_ready"], 1)

            dve.wait_ge(sem["late_loaded"], 64)
            for t in range(2):
                dve.wait_ge([sem["xt_loaded_a"], sem["xt_loaded_b"]][t], 16)
                residual(t, t, None)
                scale_rows(t, t)
            with dve.Fori(1, NT // 2) as j:
                for slot in range(2):
                    t = j * 2 + slot
                    dve.wait_ge([sem["xt_loaded_a"], sem["xt_loaded_b"]][slot], j * 16 + 16)
                    residual(t, slot, j)
                    scale_rows(t, slot)

            logits = bank(6)[:, 0:NT * E].rearrange("p (t e) -> p t e", e=E)
            ex = soft[:, 0:NT, 0:E]
            col = lambda i: stat[:, i, 0:NT]
            wide = lambda i: col(i).rearrange("p (t o) -> p t o", o=1).broadcast_to((P, NT, E))
            dve.wait_ge(sem["logits_done"], NT)
            v.tensor_reduce(col(0), logits, AX.X, ALU.max).then_inc(sem["soft_step"], 1)
            dve.wait_ge(sem["soft_step"], 1)
            v.tensor_tensor(ex, logits, wide(0), ALU.subtract).then_inc(sem["soft_step"], 1)
            dve.wait_ge(sem["exp_done"], 2)
            v.tensor_reduce(col(0), ex, AX.X, ALU.add).then_inc(sem["soft_step"], 1)
            dve.wait_ge(sem["soft_step"], 3)
            v.reciprocal(col(1), col(0)).then_inc(sem["soft_step"], 1)
            dve.wait_ge(sem["soft_step"], 4)
            v.tensor_tensor(ex, ex, wide(1), ALU.mult).then_inc(sem["soft_step"], 1)

            dve.wait_ge(sem["aff_turned"], 1)
            for i in range(2):
                dve.wait_ge(x2_stored[i], PER_SLOT)
            v.tensor_copy(aff_row[0][:], psum[0:E, 0:2, :].rearrange("p b f -> p (b f)")).then_inc(sem["aff_row_ready"], 1)
            dve.wait_ge(sem["aff_row_ready"], 1)
            for r in range(CAP // 8):
                src, dst = aff_row[r % 2], aff_row[1 - r % 2]
                best = top_val[:, 8 * r:8 * r + 8]
                v.max(best, src[:]).then_inc(sem["top_step"], 1)
                dve.wait_ge(sem["top_step"], 2 * r + 1)
                v.max_index(top_id[:, 8 * r:8 * r + 8], best, src[:])
                v.match_replace(dst[:], best, src[:], -1.0).then_inc(sem["top_step"], 1)
                dve.wait_ge(sem["top_step"], 2 * r + 2)
            v.tensor_copy(top_idf[:], top_id[:]).then_inc(sem["top_step"], 1)
            dve.wait_ge(sem["top_turned"], 1)
            v.tensor_copy(tok_id[:], bank(2)[:, 0:E]).then_inc(sem["chosen_ready"], 1)
            v.tensor_copy(gate_v[:], bank(2)[:, E:2 * E]).then_inc(sem["chosen_ready"], 1)
            dve.wait_ge(sem["chosen_ready"], 2)

            def split(e, key):
                i = at[key]
                slot = i % NS
                dve.wait_ge(sem["part_h_ready"], e * CH + i - 1)
                v.tensor_tensor(part_l[slot][:], raw[slot][:], part_h[slot][:].bitcast(F32), ALU.subtract).then_inc(sem["part_l_ready"], 1)

            def gate_up(e, f):
                dve.wait_ge(sem["silu_done"], e * NF + f + 1)
                dve.wait_ge(sem["chunk_used"], up_at(e, f))
                if not (isinstance(e, int) and e == 0 and f < 2):
                    dve.wait_ge(sem["hid_turned"], e * NF + f - 1)
                v.tensor_tensor(hid[f % 2][:], act_g[f % 2][:], bank(2 * (f % 2) + 1), ALU.mult).then_inc(sem["hid_ready"], 1)

            def turn_hidden(e, f):
                dve.wait_ge(sem["hidT_h_ready"], e * NF + f + 1)
                v.tensor_tensor(hidT_l[f % 2][:], bank(4 + f % 2).rearrange("p (k t) -> p k t", t=P), hidT_h[f % 2][:].bitcast(F32),
                                ALU.subtract).then_inc(sem["hidT_l_ready"], 1)

            def expert_out(e):
                dve.wait_ge(sem["chunk_used"], down_at(e, NF - 1))
                wait_past(dve, sem["scattered"], e * 16)
                for half in range(2):
                    cols = slice(half * HALF, (half + 1) * HALF)
                    v.scalar_tensor_tensor(y_out[:, cols], bank(6 + half), gate_v[:, bass.ds(e, 1)], gate5_row[:, cols],
                                           ALU.mult, ALU.mult).then_inc(sem["y_ready"], 1)

            def expert(e, first=False):
                if not first:
                    split(e, ("d", 3, 0))
                    split(e, ("d", 3, 1))
                    turn_hidden(e - 1, 3)
                dve.wait_ge(sem["xgT_h_ready"], e + 1)
                v.tensor_tensor(xgT_l[:], xgT[:], xgT_h[:].bitcast(F32), ALU.subtract).then_inc(sem["xgT_l_ready"], 1)
                for f in range(NF):
                    for key in (("g", f, 0), ("g", f, 1), ("u", f, 0), ("u", f, 1)):
                        split(e, key)
                    if f:
                        turn_hidden(e, f - 1)
                        split(e, ("d", f - 1, 0))
                        split(e, ("d", f - 1, 1))
                    elif not first:
                        expert_out(e - 1)
                    gate_up(e, f)

            expert(0, first=True)
            with dve.Fori(1, E) as e:
                expert(e)
            split(E, ("d", 3, 0))
            split(E, ("d", 3, 1))
            turn_hidden(E - 1, 3)
            expert_out(E - 1)

            dve.wait_ge(sem["fin_g_loaded"], 16)
            for t in range(NT):
                dve.wait_ge(sem["fin_rms"], t + 1)
                v.reciprocal(stat[:, 0, t:t + 1], stat[:, 1, t:t + 1]).then_inc(sem["fin_rstd"], 1)
                dve.wait_ge(sem["fin_rstd"], t + 1)
                v.scalar_tensor_tensor(fin_out[:, t, :], fin_in[:, t, :], stat[:, 0, t:t + 1], fin_g[:], ALU.mult, ALU.mult
                                       ).then_inc(sem["fin_ready"], 1)

        @block.tensor
        def _(pe):
            mm = nc.tensor.matmul

            def three(out_ap, pairs):
                for i, ((xh, xl), (wh, wl)) in enumerate(pairs):
                    mm(out_ap, xh, wh, start=(i == 0), stop=False)
                    mm(out_ap, xl, wh, start=False, stop=False)
                    last = mm(out_ap, xh, wl, start=False, stop=(i == len(pairs) - 1))
                return last

            pe.wait_ge(sem["small_loaded"], 16 * len(small))
            pe.wait_ge(sem["ident_ready"], 2)
            nc.tensor.transpose(bank(3)[:, 0:V_END], rows1[0:V_END, :], ident[0:V_END, 0:V_END])
            nc.tensor.transpose(bank(3)[:, P:P + TAPS * NB], rows2[0:TAPS * NB, :], ident[0:TAPS * NB, 0:TAPS * NB]
                                ).then_inc(sem["vec_turned"], 1)

            def mod_product(i):
                if i == 0:
                    pe.wait_ge(sem["silu_ready"], 1)
                pe.wait_ge(ada_sem[i % 2], 16 * (i // 2 + 1))
                if i >= 2:
                    pe.wait_ge(sem["mod_rows_ready"], i - 1)
                for k in range(KD):
                    last = mm(bank(i % 2)[0:2, :], silu_c[:, :, k], ada1[i % 2][:, k, :], start=(k == 0), stop=(k == KD - 1))
                last.then_inc(sem["mod_rows_done"], 1)

            def mod_turn(i):
                pe.wait_ge(sem["mod_rows_ready"], i + 1)
                for q in range(4):
                    last = nc.tensor.transpose(bank(2)[:, 2 * (4 * i + q):2 * (4 * i + q) + 2],
                                               mod_rows[:, i % 2, q * P:(q + 1) * P], ident[0:2, 0:2])
                last.then_inc(sem["mod_turned"], 1)

            for i in range(N_ADA1):
                mod_product(i)
                if i:
                    mod_turn(i - 1)
            mod_turn(N_ADA1 - 1)
            for n, (g, k) in enumerate(groups):
                tiles = seg_tiles[g]
                pe.wait_ge(sem["xn_ready"], tiles[-1] + 1)
                if n >= 4:
                    pe.wait_ge(sem["hf_ready"], n - 3)
                for i, t in enumerate(tiles):
                    last = nc.tensor.transpose(bank(4 + n % 4)[:, i * P:(i + 1) * P], xbuf[:, t, k * P:(k + 1) * P], ident[:])
                last.then_inc(sem["x_turned"], 1)

            pe.wait_ge(sem["hf_ready"], len(groups))
            pe.wait_ge(sem["mod_col_ready"], 1)
            pe.wait_ge(sem["hT_l_ready"], len(groups))

            def mixer_block(n, slot, ada):
                wh, wl, gh, gl = win_h[slot], win_l[slot], gatew_h[slot], gatew_l[slot]
                project = lambda out_ap, c0, lo, w: three(out_ap, [
                    ((wh[:, k, c0:c0 + P], wl[:, k, c0:c0 + P]), (hT_h[:, k, lo:lo + w], hT_l[:, k, lo:lo + w])) for k in range(KD)])
                pe.wait_ge(sem["win_l_ready"], n + 1)
                wait_past(pe, sem["conv_done"], n * 6)
                for lo, w in SEGS:
                    last = project(pu[:, lo:lo + w], P, lo, w)
                last.then_inc(sem["u_done"], 1)
                if ada:
                    pe.wait_ge(sem["ada_chunk_loaded"], n * 32 + 32)
                    wait_past(pe, sem["sig_done"], n * 12)
                    for k in range(KD):
                        last = mm(bank(7)[0:1, :], silu_c[:, 0, k:k + 1], ada_buf[:, k, :], start=(k == 0), stop=(k == KD - 1))
                    last.then_inc(sem["ada_done"], 1)
                wait_past(pe, sem["gelu_done"], n)
                for half in range(2):
                    last = project(bank(3 + half), 0, half * HALF, HALF)
                last.then_inc(sem["g_done"], 1)
                pe.wait_ge(sem["u_l_ready"], n + 1)
                if ada:
                    pe.wait_ge(sem["ada_out"], n + 1)
                for m in range(4):
                    d, is_i = divmod(m, 2)
                    q = 2 * is_i + d
                    for g, (lo, w) in enumerate(SEGS):
                        if m == 0:
                            wait_past(pe, sem["sig_done"], n * 12)
                        else:
                            pe.wait_ge(sem["sig_done"], n * 12 + 3 * (m - 1) + g + 1)
                        three(bank(5 + g)[:, 0:w], [((gh[:, q, :], gl[:, q, :]), (u_h[:, lo:lo + w], u_l[:, lo:lo + w]))]
                              ).then_inc(sem["gate_done"], 1)

            mixer_block(0, 0, True)
            mixer_block(1, 1, True)
            with pe.Fori(1, NB // 2 - 1) as j:
                mixer_block(j * 2, 0, True)
                mixer_block(j * 2 + 1, 1, True)
            mixer_block(NB - 2, 0, False)
            mixer_block(NB - 1, 1, False)

            pe.wait_ge(sem["late_loaded"], 64)
            pe.wait_ge(sem["sig_done"], 12 * NB)
            nc.tensor.transpose(bank(7)[:, 0:2 * KD], rows3[:], ident[0:2 * KD, 0:2 * KD]).then_inc(sem["rows3_turned"], 1)

            def project_out(t, slot, uses, first):
                pe.wait_ge([sem["yt_loaded_a"], sem["yt_loaded_b"]][slot], uses)
                for half in range(2):
                    if not first:
                        pe.wait_ge(sem["gated_done"], (t - 1) * 2)
                    cols = slice(half * HALF, (half + 1) * HALF)
                    three(bank(2 * slot + half), [((yt_h[slot][:, n, :], yt_l[slot][:, n, :]), (wo_h[:, n, cols], wo_l[:, n, cols]))
                                                  for n in range(NB)]).then_inc(sem["proj_done"], 1)

            def turn_tile(t, slot):
                pe.wait_ge(sem["xn2_ready"], t + 1)
                wait_past(pe, sem["h2T_ready"], t)
                for k in range(KD):
                    last = nc.tensor.transpose(bank(4 + k // 4)[:, (k % 4) * P:(k % 4 + 1) * P], xn[slot][:, k * P:(k + 1) * P], ident[:])
                last.then_inc(sem["xn_turned"], 1)

            def route(t):
                pe.wait_ge(sem["h2T_ready"], t + 1)
                for k in range(KD):
                    last = mm(bank(6)[:, bass.ds(t * E, E)], h2T[:, k, :], router[:, k, :], start=(k == 0), stop=(k == KD - 1))
                last.then_inc(sem["logits_done"], 1)

            pe.wait_ge(sem["wo_l_ready"], NB // 2)
            pe.wait_ge(sem["y_done"], NB)
            project_out(0, 0, 32, True)
            project_out(1, 1, 32, True)
            turn_tile(0, 0)
            with pe.Fori(1, NT // 2) as j:
                for slot in range(2):
                    t = j * 2 + slot
                    project_out(t, slot, j * 32 + 32, False)
                    route(t - 2)
                    turn_tile(t - 1, 1 - slot)
            route(NT - 2)
            turn_tile(NT - 1, 1)
            route(NT - 1)

            pe.wait_ge(sem["soft_step"], 5)
            for t in range(NT):
                last = nc.tensor.transpose(psum[0:E, t // 4, (t % 4) * P:(t % 4 + 1) * P], soft[:, t, 0:E], ident[:])
            last.then_inc(sem["aff_turned"], 1)
            pe.wait_ge(sem["top_step"], 2 * (CAP // 8) + 1)
            nc.tensor.transpose(bank(2)[:, 0:E], top_idf[:], ident[0:E, 0:E])
            nc.tensor.transpose(bank(2)[:, E:2 * E], top_val[:], ident[0:E, 0:E]).then_inc(sem["top_turned"], 1)

            def weights(kind, slot):
                n = 2 if kind == "d" else 4
                r = lambda ap: ap[:].rearrange("p (k f) -> p k f", k=n)
                return r(part_h[slot]), r(part_l[slot])

            def in_product(e, kind, f):
                dst = bank(2 * (f % 2) + (kind == "u"))
                if not (isinstance(e, int) and e == 0 and f < 2):
                    pe.wait_ge(sem["hid_ready"], e * NF + f - 1)
                for half in range(2):
                    key = (kind, f, half)
                    wh, wl = weights(kind, at[key] % NS)
                    pe.wait_ge(sem["part_l_ready"], used(e, key))
                    for k in range(4):
                        kk = 4 * half + k
                        mm(dst, xgT_h[:, kk, :], wh[:, k, :], start=(kk == 0), stop=False)
                        mm(dst, xgT_l[:, kk, :], wh[:, k, :], start=False, stop=False)
                        last = mm(dst, xgT_h[:, kk, :], wl[:, k, :], start=False, stop=(kk == KD - 1))
                    if half == 0:
                        last.then_inc(sem["chunk_used"], 1)
                last.then_inc(sem["chunk_used"], 1)

            def turn_hidden(e, f):
                pe.wait_ge(sem["hid_ready"], e * NF + f + 1)
                for k in range(4):
                    last = nc.tensor.transpose(bank(4 + f % 2)[:, k * P:(k + 1) * P], hid[f % 2][:, k * P:(k + 1) * P], ident[:])
                last.then_inc(sem["hid_turned"], 1)

            def down_product(e, f, e_at):
                pe.wait_ge(sem["hidT_l_ready"], e * NF + f + 1)
                if f == 0:
                    wait_past(pe, sem["y_ready"], e * 2)
                for half in range(2):
                    key = ("d", f, half)
                    wh, wl = weights("d", at[key] % NS)
                    pe.wait_ge(sem["part_l_ready"], used(e_at, key))
                    for k in range(2):
                        kk = 2 * half + k
                        for n in range(2):
                            cols = slice(n * HALF, (n + 1) * HALF)
                            first, final = f == 0 and kk == 0, f == NF - 1 and kk == 3
                            mm(bank(6 + n), hidT_h[f % 2][:, kk, :], wh[:, k, cols], start=first, stop=False)
                            mm(bank(6 + n), hidT_l[f % 2][:, kk, :], wh[:, k, cols], start=False, stop=False)
                            last = mm(bank(6 + n), hidT_h[f % 2][:, kk, :], wl[:, k, cols], start=False, stop=final)
                    if half == 0:
                        last.then_inc(sem["chunk_used"], 1)
                last.then_inc(sem["chunk_used"], 1)

            def turn_rows(e, first):
                pe.wait_ge(sem["gathered"], e * 16 + 16)
                for half in range(2):
                    if not first and half == 0:
                        pe.wait_ge(sem["hid_ready"], e * NF - 1)
                    for k in range(4):
                        kk = 4 * half + k
                        last = nc.tensor.transpose(bank(half)[:, k * P:(k + 1) * P], xg[:, kk * P:(kk + 1) * P], ident[:])
                    last.then_inc(sem["xg_turned"], 1)

            def expert(e, first=False):
                if not first:
                    turn_hidden(e - 1, 3)
                turn_rows(e, first)
                if not first:
                    down_product(e - 1, 3, e)
                pe.wait_ge(sem["xgT_l_ready"], e + 1)
                for f in range(NF):
                    in_product(e, "g", f)
                    if f:
                        turn_hidden(e, f - 1)
                    in_product(e, "u", f)
                    if f:
                        down_product(e, f - 1, e)

            expert(0, first=True)
            with pe.Fori(1, E) as e:
                expert(e)
            turn_hidden(E - 1, 3)
            down_product(E - 1, 3, E)


def build(nc, **arrays):
    with ExitStack() as stack:
        program(nc, stack, **arrays)


_INS = ['x', 'c', 'ctx', 'c_ctx', 'ada_w', 'ada_b', 'norm_mix_g', 'norm_ffn_g', 'final_g', 'a_w_in', 'a_conv_w',
        'a_conv_b', 'a_gate_wa', 'a_gate_ba', 'a_gate_wx', 'a_gate_bx', 'a_lambda', 'a_w_out', 'router_w',
        'exp_w_gate', 'exp_w_up', 'exp_w_down']


def kernel(**inputs):
    import numpy as _np
    import concourse.bacc as _bacc
    from concourse import mybir as _mybir
    from concourse.bass_utils import run_bass_kernel_spmd as _run

    nc = _bacc.Bacc("TRN2", target_bir_lowering=False, num_devices=1)
    arrays, args = {}, {}
    for name in _INS:
        a = _np.ascontiguousarray(inputs[name])
        arrays[f"in_{name}_dram"] = a
        args[name] = nc.dram_tensor(f"in_{name}_dram", a.shape, _mybir.dt.from_np(a.dtype), kind="ExternalInput").ap()
    out = nc.dram_tensor("out_0_dram", inputs["x"].shape, _mybir.dt.float32, kind="ExternalOutput").ap()
    build(nc, out=out, **args)
    r = _run(nc, [arrays], core_ids=[0])
    return r.results[0]["out_0_dram"]
```

```python
from contextlib import ExitStack

import concourse.bass as bass
from concourse import mybir

F32 = mybir.dt.float32
F32R = mybir.dt.float32r
I32 = mybir.dt.int32
U32 = mybir.dt.uint32
ALU = mybir.AluOpType
ACT = mybir.ActivationFunctionType
AX = mybir.AxisListType
KB = 1024


def program(nc, stack, x, c, ctx, c_ctx, ada_w, ada_b, norm_mix_g, norm_ffn_g, final_g, a_w_in, a_conv_w,
            a_conv_b, a_gate_wa, a_gate_ba, a_gate_wx, a_gate_bx, a_lambda, a_w_out, router_w,
            exp_w_gate, exp_w_up, exp_w_down, out):
    P = 128
    SEQ, D = x.shape[1:]
    CTX = ctx.shape[1]
    KD = D // P
    NT = SEQ // P
    NCT = CTX // P
    LEN = SEQ + CTX
    D_RNN = a_w_out.shape[1]
    NB = D_RNN // P
    GRID_W = 64
    ROWS = SEQ // GRID_W
    TAPS, CENTRE = 4, 2
    E = router_w.shape[2]
    CAP = 2 * SEQ // E
    FF = exp_w_gate.shape[3]
    HALF = 512
    NF = FF // HALF
    EPS = 1e-6
    RG_C = 8.0
    assert CAP == P and KD * LEN == NB * D and NF == 4
    SEGS = [(0, HALF), (HALF, HALF), (SEQ, CTX)]

    base = nc.sbuf_base
    base += -base % 64

    def place(name, shape, dtype, kb):
        return nc.alloc_sbuf_tensor_at(name, shape, dtype, offset=base + int(kb * KB))

    act_h = place("act_h", [P, KD * LEN], F32R, 0)
    act_l = place("act_l", [P, KD * LEN], F32R, 40)
    hT_h = act_h[:].rearrange("p (k t) -> p k t", k=KD)
    hT_l = act_l[:].rearrange("p (k t) -> p k t", k=KD)
    wo_h = act_h[:].rearrange("p (n d) -> p n d", n=NB)
    wo_l = act_l[:].rearrange("p (n d) -> p n d", n=NB)
    win_raw = place("win_raw", [P, KD, 2 * P], F32, 80)
    gate_raw = place("gate_raw", [P, 4, P], F32, 88)
    win_h = [place(f"win_h{s}", [P, KD, 2 * P], F32R, 90 + 20 * s) for s in range(2)]
    win_l = [place(f"win_l{s}", [P, KD, 2 * P], F32R, 98 + 20 * s) for s in range(2)]
    gatew_h = [place(f"gatew_h{s}", [P, 4, P], F32R, 106 + 20 * s) for s in range(2)]
    gatew_l = [place(f"gatew_l{s}", [P, 4, P], F32R, 108 + 20 * s) for s in range(2)]
    ada_piece = place("ada_piece", [P, 2, HALF], F32, 130)
    u = place("u", [P, LEN], F32, 134)
    u_h = place("u_h", [P, LEN], F32R, 139)
    u_l = place("u_l", [P, LEN], F32R, 144)
    r_d = [place("r_fwd", [P, LEN], F32, 149), place("r_bwd", [P, LEN], F32, 159)]
    i_d = [place("i_fwd", [P, LEN], F32, 154), place("i_bwd", [P, LEN], F32, 164)]
    a_d = [place("a_fwd", [P, LEN], F32, 169), place("a_bwd", [P, LEN], F32, 179)]
    t_d = [place("t_fwd", [P, LEN], F32, 174), place("t_bwd", [P, LEN], F32, 184)]
    y = place("y", [P, SEQ], F32, 189)
    y_h = place("y_h", [P, SEQ], F32R, 193)
    y_l = place("y_l", [P, SEQ], F32R, 197)
    mod_out = place("mod_out", [1, HALF], F32, 201)
    ada_sum = place("ada_sum", [P, HALF], F32, 203)
    wo_raw = [win_raw] + [place(f"wo_raw{s}", [P, KD, 2 * P], F32, kb) for s, kb in ((1, 90), (2, 98), (3, 110), (4, 118))]
    xbuf = place("xbuf", [P, NT + NCT, D], F32, 146)
    ada1 = [place(f"ada_buf{i}", [P, KD, HALF], F32, kb) for i, kb in enumerate((130, 110, 0, 16))]
    mod_rows = place("mod_rows", [2, 2, HALF], F32, 186)
    junk = place("junk", [P, D], F32, 191)
    NH = 4
    hf = place("hf", [P, NH, HALF], F32, 195)
    SM = 205
    ident = place("ident", [P, P], F32, SM)
    vec1 = place("vec1", [P, 120], F32, SM + 0.5)
    taps = place("taps", [P, TAPS * NB], F32, SM + 1)
    silu_c = place("silu_c", [P, 2, KD], F32, SM + 1.1875)
    rate = place("rate", [P, 2, 20], F32, SM + 1.25)
    mod_col = place("mod_col", [P, 2, 16], F32, SM + 1.4375)
    scale1 = place("scale1", [P, 2, KD], F32, SM + 1.5625)
    scale2 = place("scale2", [P, KD], F32, SM + 1.625)
    shift2 = place("shift2", [P, KD], F32, SM + 1.65625)
    eps = place("eps", [P, 1], F32, SM + 1.6875)
    ones = place("ones", [P, 1], F32, SM + 2.8125)
    stat = place("stat", [P, 2, 12], F32, SM + 1.71875)
    tok_id = place("tok_id", [P, E], I32, SM + 1.8125)
    gate_v = place("gate_v", [P, E], F32, SM + 1.875)
    block_col = [place(f"block_col{s}", [P, 13], F32, SM + 2.6875 + s * 0.0625) for s in range(2)]
    id_gather = place("id_gather", [P, 1], I32, SM + 1.9375)
    id_scatter = place("id_scatter", [P, 1], I32, SM + 1.96875)
    soft = place("soft", [P, 8, 20], F32, SM + 2)
    rows1 = place("rows1", [P, P], F32, 203)
    rows2 = place("rows2", [P, P], F32, 203.5)
    yt_h = [place(f"yt_h{s}", [P, NB, P], F32R, 146 + 10 * s) for s in range(2)]
    yt_l = [place(f"yt_l{s}", [P, NB, P], F32R, 151 + 10 * s) for s in range(2)]
    xt = [place(f"xt{s}", [P, D], F32, 166 + 4 * s) for s in range(2)]
    x2 = [place(f"x2_{s}", [P, D], F32, 174 + 4 * s) for s in range(2)]
    xn = [place(f"xn{s}", [P, D], F32, 182 + 4 * s) for s in range(2)]
    h2T = place("h2T", [P, KD, P], F32, 190)
    gate2_row = place("gate2_row", [P, D], F32, 84)
    gate5_row = place("gate5_row", [P, D], F32, 199)
    router = place("router", [P, KD, E], F32, 88)
    rows3 = place("rows3", [2 * KD, P], F32, 88.5)
    aff_row = [place(f"aff_row{s}", [E, SEQ], F32, 166 + 4 * s) for s in range(2)]
    top_val = place("top_val", [E, CAP], F32, 174)
    top_id = place("top_id", [E, CAP], U32, 174.5)
    top_idf = place("top_idf", [E, CAP], F32, 175)
    NS = 6
    part_h = [place(f"part_h{s}", [P, 4 * HALF], F32R, 16 * s) for s in range(NS)]
    part_l = [place(f"part_l{s}", [P, 4 * HALF], F32R, 16 * s + 8) for s in range(NS)]
    raw = [place(f"raw{s}", [P, 4 * HALF], F32, 96 + 8 * s) for s in range(NS)]
    xg = place("xg", [P, D], F32, 146)
    xgT = place("xgT", [P, KD, P], F32, 150)
    xgT_h = place("xgT_h", [P, KD, P], F32R, 154)
    xgT_l = place("xgT_l", [P, KD, P], F32R, 158)
    act_g = [place(f"act_g{s}", [P, HALF], F32, 162 + 2 * s) for s in range(2)]
    hid = [place(f"hid{s}", [P, HALF], F32, 176 + 2 * s) for s in range(2)]
    hidT_h = [place(f"hidT_h{s}", [P, 4, P], F32R, 180 + 4 * s) for s in range(2)]
    hidT_l = [place(f"hidT_l{s}", [P, 4, P], F32R, 182 + 4 * s) for s in range(2)]
    y_out = place("y_out", [P, D], F32, 188)
    fin_in = place("fin_in", [P, NT, D], F32, 0)
    fin_out = place("fin_out", [P, NT, D], F32, 32)
    fin_g = place("fin_g", [P, D], F32, 64)
    fin_junk = place("fin_junk", [P, D], F32, 68)
    assert base + (SM + 2.8125 + 0.03125) * KB <= nc.sbuf_usable_end

    psum = nc.alloc_psum_tensor("psum", [P, 8, HALF], F32)
    pu = psum[:, 0:3, :].rearrange("p b f -> p (b f)")
    bank = lambda b: psum[:, b, :]

    y_scr = nc.dram_tensor("y_scr", [2, NB, P, SEQ], F32).ap()
    x_scr = nc.dram_tensor("x_scr", [SEQ, D], F32).ap()
    n_scr = nc.dram_tensor("n_scr", [SEQ, D], F32).ap()
    mod_scr = nc.dram_tensor("mod_scr", [4 * D], F32).ap()

    ada_v = ada_w[0].rearrange("(k p) f -> p k f", p=P)
    win_v = a_w_in[0].rearrange("(k p) f -> p k f", p=P)
    wo_v = a_w_out[0].rearrange("(n p) d -> p n d", p=P)
    wa_v = a_gate_wa[0].rearrange("d n c e -> n c d e")
    wx_v = a_gate_wx[0].rearrange("d n c e -> n c d e")
    wg_v = exp_w_gate[0].rearrange("e (k p) f -> e p k f", p=P)
    wu_v = exp_w_up[0].rearrange("e (k p) f -> e p k f", p=P)
    wd_v = exp_w_down[0].rearrange("e (k p) f -> e p k f", p=P)

    names = """small_loaded ident_ready   vec_turned vec_ready
        silu_ready mod_rows_done mod_rows_ready mod_turned mod_col_ready softplus_step squares_done rms_done
        rstd_ready xn_ready x_turned hf_ready hT_h_ready hT_l_ready
        win_loaded win_h_ready win_l_ready u_done g_done gate_done conv_init conv_done u_h_ready
        u_l_ready gelu_done sig_done a_done t_done v_done q_done w_done s_done b_done scan_ctx
        scan_done y_sum y_done y_h_ready y_l_ready y_stored  ada_done
        ada_out mod_stored  wo_h_ready wo_l_dve wo_l_pool late_loaded gate5_loaded rows3_turned mod2_step
        yt_loaded_a yt_loaded_b xt_loaded_a xt_loaded_b proj_done gated_done x2_ready sq2_done
        rms2_done rstd2_ready xn2_ready xn_turned h2T_ready logits_done
        soft_step exp_done aff_turned aff_row_ready top_step top_turned chosen_ready
        id_ready first_id_ready gathered xg_turned xgT_ready xgT_h_ready xgT_l_ready part_h_ready part_l_ready
        chunk_used silu_done hid_ready hid_turned hidT_h_ready hidT_l_ready
        y_ready id2_ready scattered fin_g_loaded fin_sq fin_rms fin_rstd
        fin_ready fin_stored bias_loaded piece_scaled piece_used""".split()
    piece_loaded = [stack.enter_context(nc.semaphore(f"piece_loaded{i}")) for i in range(2)]
    raw_loaded = [stack.enter_context(nc.semaphore(f"raw_loaded{i}")) for i in range(NS)]

    x_loaded = [stack.enter_context(nc.semaphore(f"x_loaded{t}")) for t in range(NT + NCT)]
    fin_loaded = [stack.enter_context(nc.semaphore(f"fin_loaded{t}")) for t in range(NT)]
    x2_stored = [stack.enter_context(nc.semaphore(f"x2_stored{i}")) for i in range(2)]
    n_stored = [stack.enter_context(nc.semaphore(f"n_stored{i}")) for i in range(2)]
    PER_SLOT = 16 * NT // 2

    sem = {n: stack.enter_context(nc.semaphore(n)) for n in names}

    V_ADA, V_NM, V_NF, V_CB, V_BA, V_BX, V_LAM, V_C = 0, 16, 24, 32, 42, 62, 82, 102
    V_END = V_C + 2 * KD
    as_rows = lambda ap, pat: ap.rearrange(pat, q=P)
    small = [
        (rows1, V_ADA, as_rows(ada_b[0, 0:2 * D], "(r q) -> r q"), 2 * KD),
        (rows1, V_NM, as_rows(norm_mix_g[0], "(r q) -> r q"), KD),
        (rows1, V_NF, as_rows(norm_ffn_g[0], "(r q) -> r q"), KD),
        (rows1, V_CB, as_rows(a_conv_b[0], "(r q) -> r q"), NB),
        (rows1, V_BA, as_rows(a_gate_ba[0], "d (r q) -> (d r) q"), 2 * NB),
        (rows1, V_BX, as_rows(a_gate_bx[0], "d (r q) -> (d r) q"), 2 * NB),
        (rows1, V_LAM, as_rows(a_lambda[0], "d (r q) -> (d r) q"), 2 * NB),
        (rows1, V_C, as_rows(c[0], "(r q) -> r q"), KD),
        (rows1, V_C + KD, as_rows(c_ctx, "(r q) -> r q"), KD),
        (rows2, 0, as_rows(a_conv_w[0], "j (r q) -> (j r) q"), TAPS * NB),
    ]
    N_ADA1 = 2 * D // HALF
    N_ADA2 = 4 * D // HALF
    WO_DVE = 3
    ADA_EARLY = 6
    ada_loaded = [stack.enter_context(nc.semaphore(f"ada_loaded{i}")) for i in range(N_ADA1)]
    wo_loaded = [stack.enter_context(nc.semaphore(f"wo_loaded{i}")) for i in range(NB // 2)]
    seg_tiles = [range(0, 4), range(4, 8), range(NT, NT + NCT)]
    groups = [(g, k) for g in range(3) for k in range(KD)]

    order = [("d", 3, 0), ("d", 3, 1)]
    for f in range(NF):
        order += [("g", f, 0), ("g", f, 1), ("u", f, 0), ("u", f, 1)]
        if f:
            order += [("d", f - 1, 0), ("d", f - 1, 1)]
    CH = len(order)
    assert CH % NS == 0
    at = {key: i for i, key in enumerate(order)}
    used = lambda e, key: e * CH + at[key] - 1
    gate_at = lambda e, f: used(e, ("g", f, 1))
    up_at = lambda e, f: used(e, ("u", f, 1))
    down_at = lambda e, f: used(e + 1 if f == NF - 1 else e, ("d", f, 1))
    two_before = lambda e, f: (e, f - 2) if f >= 2 else (e - 1, f - 2 + NF)

    def wait_past(eng, signal, value):
        if not (isinstance(value, int) and value <= 0):
            eng.wait_ge(signal, value)

    with nc.Block() as block:

        @block.sync
        def _(sp):
            for dst, row, src, n in small:
                sp.dma_start(dst[row:row + n, :], src).then_inc(sem["small_loaded"], 16)

            def load_ada1(i):
                sp.dma_start(ada1[i][:], ada_v[:, :, i * HALF:(i + 1) * HALF]).then_inc(ada_loaded[i], 16)

            def load_x(t):
                src = x[0, t * P:(t + 1) * P, :] if t < NT else ctx[0, (t - NT) * P:(t - NT + 1) * P, :]
                sp.dma_start(xbuf[:, t, :], src).then_inc(x_loaded[t], 16)

            def load_block(n):
                sp.dma_start(win_raw[:, :, 0:P], win_v[:, :, bass.ds(n * P, P)]).then_inc(sem["win_loaded"], 16)
                sp.dma_start(win_raw[:, :, P:2 * P], win_v[:, :, bass.ds(n * P + D_RNN, P)]).then_inc(sem["win_loaded"], 16)
                sp.dma_start(gate_raw[:, 0:2, :], wa_v[bass.ds(n, 1)].rearrange("o c d e -> (o c) d e")).then_inc(sem["win_loaded"], 16)
                sp.dma_start(gate_raw[:, 2:4, :], wx_v[bass.ds(n, 1)].rearrange("o c d e -> (o c) d e")).then_inc(sem["win_loaded"], 16)

            def load_ada2(n):
                for k in range(KD):
                    wait_past(sp, sem["piece_used"], n * KD + k - 1)
                    sp.dma_start(ada_piece[:, k % 2, :], ada_v[:, k, bass.ds(n * HALF + 2 * D, HALF)]).then_inc(piece_loaded[k % 2], 16)

            def load_bias(n):
                wait_past(sp, sem["mod_stored"], n * 16)
                sp.dma_start(mod_out[:], ada_b[0:1, bass.ds(n * HALF + 2 * D, HALF)]).then_inc(sem["bias_loaded"], 16)

            load_ada1(0)
            for t in range(0, 4):
                load_x(t)
            for i in range(1, N_ADA1):
                load_ada1(i)
            load_block(0)
            for t in range(4, NT + NCT):
                load_x(t)

            def block_loads(n):
                sp.wait_ge(sem["win_h_ready"], n)
                sp.wait_ge(sem["win_l_ready"], n)
                load_block(n)

            block_loads(1)
            sp.wait_ge(sem["mod_rows_done"], N_ADA1)
            load_ada2(0)
            sp.wait_ge(sem["hT_l_ready"], len(groups))
            load_bias(0)
            with sp.Fori(2, N_ADA2 + 1) as n:
                block_loads(n)
                load_ada2(n - 1)
                load_bias(n - 1)
            for n in range(N_ADA2 + 1, NB):
                block_loads(n)

            for i in range(NB // 2):
                if i == 0:
                    sp.wait_ge(sem["win_h_ready"], NB)
                    sp.wait_ge(sem["win_l_ready"], NB)
                elif i == 1:
                    sp.wait_ge(sem["gate_done"], 12 * (NB - 1))
                elif i == 3:
                    sp.wait_ge(sem["g_done"], NB)
                sp.dma_start(wo_raw[i][:].rearrange("p k f -> p (k f)").rearrange("p (n d) -> p n d", n=2),
                             wo_v[:, 2 * i:2 * i + 2, :]).then_inc(wo_loaded[i], 16)
            row_of = lambda ap: ap.rearrange("(o f) -> o f", o=1).broadcast_to((P, D))

            sp.wait_ge(sem["mod_stored"], 16 * N_ADA2)
            sp.wait_ge(sem["wo_l_dve"], 1)
            sp.dma_start(gate2_row[:], row_of(mod_scr[0:D])).then_inc(sem["late_loaded"], 16)
            sp.dma_start(rows3[:], mod_scr[D:3 * D].rearrange("(r q) -> r q", q=P)).then_inc(sem["late_loaded"], 16)
            sp.dma_start(router[:], router_w[0].rearrange("(k p) e -> p k e", p=P)).then_inc(sem["late_loaded"], 16)

            def tile_loads(t, slot, first):
                if first:
                    sp.wait_ge(sem["b_done"], 2 * NB)
                else:
                    sp.wait_ge(sem["proj_done"], (t - 1) * 2)
                    sp.wait_ge(sem["x2_ready"], t - 1)
                cols = bass.ds(t * P, P)
                blocks = NB - 1 if first else NB
                yt_loaded = [sem["yt_loaded_a"], sem["yt_loaded_b"]][slot]
                for part, dst in enumerate((yt_h, yt_l)):
                    sp.dma_start(dst[slot][:, 0:blocks, :].bitcast(F32), y_scr[part, 0:blocks].rearrange("n c t -> c n t")[:, :, cols]
                                 ).then_inc(yt_loaded, 16)
                if first:
                    sp.wait_ge(sem["scan_done"], 2 * NB)
                    sp.wait_ge(sem["y_sum"], NB)
                sp.dma_start(xt[slot][:], x[0, cols, :]).then_inc([sem["xt_loaded_a"], sem["xt_loaded_b"]][slot], 16)

            def tile_stores(t, slot):
                rows = bass.ds(t * P, P)
                sp.wait_ge(sem["x2_ready"], t + 1)
                sp.dma_start(x_scr[rows, :], x2[slot][:]).then_inc(x2_stored[slot], 16)
                sp.wait_ge(sem["xn2_ready"], t + 1)
                sp.dma_start(n_scr[rows, :], xn[slot][:]).then_inc(n_stored[slot], 16)

            sp.wait_ge(sem["y_stored"], 32 * (NB - 1))
            for t in range(2):
                tile_loads(t, t, True)
            sp.wait_ge(sem["y_stored"], 32 * NB)
            with sp.Fori(0, NT // 2 - 1) as j:
                for slot in range(2):
                    tile_stores(j * 2 + slot, slot)
                    tile_loads(j * 2 + slot + 2, slot, False)

            def load_chunk(e, i, first=False):
                kind, f, half = order[i]
                slot = i % NS
                if kind == "d":
                    e_of = e - 1 if f == NF - 1 else e
                    src = wd_v[bass.ds(e_of, 1), :, 4 * f + 2 * half:4 * f + 2 * half + 2, :]
                    dst = raw[slot][:].rearrange("p (k f) -> p k f", k=2)
                else:
                    src = (wg_v if kind == "g" else wu_v)[bass.ds(e, 1), :, 4 * half:4 * half + 4, f * HALF:(f + 1) * HALF]
                    dst = raw[slot][:].rearrange("p (k f) -> p k f", k=4)
                if not first:
                    sp.wait_ge(sem["part_h_ready"], e * CH + i - NS - 1)
                    sp.wait_ge(sem["part_l_ready"], e * CH + i - NS - 1)
                sp.dma_start(dst, src.rearrange("o p k f -> (o p) k f")).then_inc(raw_loaded[slot], 16)

            sp.wait_ge(sem["wo_l_dve"], WO_DVE)
            sp.wait_ge(sem["wo_l_pool"], NB // 2 - WO_DVE)
            sp.wait_ge(sem["gate_done"], 12 * NB)
            for i in range(2, 2 + NS):
                load_chunk(0, i, first=True)
            for t in range(NT - 2, NT):
                tile_stores(t, t % 2)
            sp.dma_start(gate5_row[:], row_of(mod_scr[3 * D:4 * D])).then_inc(sem["gate5_loaded"], 16)
            for i in range(2 + NS, CH):
                load_chunk(0, i)
            with sp.Fori(1, E) as e:
                for i in range(CH):
                    load_chunk(e, i)
            for i in range(2):
                load_chunk(E, i)

            sp.wait_ge(sem["chunk_used"], E * CH)
            sp.dma_start(fin_g[:], row_of(final_g)).then_inc(sem["fin_g_loaded"], 16)
            sp.wait_ge(sem["scattered"], 16 * E)
            for t in range(NT):
                sp.dma_start(fin_in[:, t, :], x_scr[t * P:(t + 1) * P, :]).then_inc(fin_loaded[t], 16)
            for t in range(NT):
                sp.wait_ge(sem["fin_ready"], t + 1)
                sp.dma_start(out[0, t * P:(t + 1) * P, :], fin_out[:, t, :]).then_inc(sem["fin_stored"], 16)
            sp.wait_ge(sem["fin_stored"], 16 * NT)
            for i in range(2):
                sp.wait_ge(x2_stored[i], PER_SLOT)
                sp.wait_ge(n_stored[i], PER_SLOT)

        @block.gpsimd
        def _(pool):
            nc.gpsimd.memset(ident[:], 0.0).then_inc(sem["ident_ready"], 1)
            nc.gpsimd.memset(ones[:], 1.0)
            nc.gpsimd.memset(eps[:], EPS)
            pool.wait_ge(sem["ident_ready"], 1)
            nc.gpsimd.affine_select(out=ident[:], in_=ident[:], compare_op=ALU.not_equal, fill=1.0, base=0,
                                    pattern=[[-1, P]], channel_multiplier=1).then_inc(sem["ident_ready"], 1)

            for n, (g, k) in enumerate(groups):
                lo, w = SEGS[g]
                pool.wait_ge(sem["hf_ready"], n + 1)
                nc.gpsimd.tensor_scalar(hT_h[:, k, lo:lo + w], hf[:, n % NH, 0:w], 1.0, 0.0, ALU.mult, ALU.add
                                        ).then_inc(sem["hT_h_ready"], 1)

            def ada_sums(n, lo, hi):
                for k in range(lo, hi):
                    slot = k % 2
                    piece, col = ada_piece[:, slot, :], silu_c[:, 0, k:k + 1].broadcast_to((P, HALF))
                    pool.wait_ge(piece_loaded[slot], (n * (KD // 2) + k // 2 + 1) * 16)
                    if k == 0:
                        wait_past(pool, sem["ada_done"], n)
                        nc.gpsimd.tensor_tensor(ada_sum[:], piece, col, ALU.mult).then_inc(sem["piece_used"], 1)
                    else:
                        nc.gpsimd.tensor_tensor(piece, piece, col, ALU.mult).then_inc(sem["piece_scaled"], 1)
                        pool.wait_ge(sem["piece_scaled"], n * (KD - 1) + k)
                        pool.wait_ge(sem["piece_used"], n * KD + k)
                        nc.gpsimd.tensor_tensor(ada_sum[:], ada_sum[:], piece, ALU.add).then_inc(sem["piece_used"], 1)

            def coefficients(n):
                for d in range(2):
                    pool.wait_ge(sem["sig_done"], n * 12 + 6 * d + 6)
                    nc.gpsimd.tensor_tensor(i_d[d][:], i_d[d][:], u[:], ALU.mult).then_inc(sem["v_done"], 1)

            def store_y(n):
                for part, (buf, ready) in enumerate(((y_h, sem["y_h_ready"]), (y_l, sem["y_l_ready"]))):
                    pool.wait_ge(ready, n + 1)
                    pool.dma_start(y_scr[part, bass.ds(n, 1)].rearrange("o c t -> (o c) t"), buf[:].bitcast(F32)).then_inc(sem["y_stored"], 16)

            def store_mod(n):
                pool.wait_ge(sem["ada_out"], n + 1)
                pool.dma_start(mod_scr[bass.ds(n * HALF, HALF)].rearrange("(o f) -> o f", o=1), mod_out[:]).then_inc(sem["mod_stored"], 16)

            ada_sums(0, 0, ADA_EARLY)
            coefficients(0)
            ada_sums(0, ADA_EARLY, KD)
            with pool.Fori(1, N_ADA2) as n:
                ada_sums(n, 0, ADA_EARLY)
                coefficients(n)
                store_y(n - 1)
                store_mod(n - 1)
                ada_sums(n, ADA_EARLY, KD)
            def wo_high(i):
                pool.wait_ge(sem["g_done"], NB)
                pool.wait_ge(wo_loaded[i], 16)
                nc.gpsimd.tensor_scalar(act_h[:, 2 * i * D:(2 * i + 2) * D], wo_raw[i][:].rearrange("p k f -> p (k f)"),
                                        1.0, 0.0, ALU.mult, ALU.add).then_inc(sem["wo_h_ready"], 1)

            for n in range(N_ADA2, NB):
                if n == NB - 1:
                    for i in range(WO_DVE):
                        wo_high(i)
                coefficients(n)
                if n == NB - 1:
                    for i in range(WO_DVE, NB // 2):
                        wo_high(i)
                store_y(n - 1)
                if n == N_ADA2:
                    store_mod(n - 1)

            for i in range(WO_DVE, NB // 2):
                pool.wait_ge(sem["wo_h_ready"], i + 1)
                cols = slice(2 * i * D, (2 * i + 2) * D)
                nc.gpsimd.tensor_tensor(act_l[:, cols], wo_raw[i][:].rearrange("p k f -> p (k f)"), act_h[:, cols].bitcast(F32),
                                        ALU.subtract).then_inc(sem["wo_l_pool"], 1)
            store_y(NB - 1)

            for i in range(2, 2 + NS):
                slot = i % NS
                pool.wait_ge(sem["part_h_ready"], i - 1)
                nc.gpsimd.tensor_tensor(part_l[slot][:], raw[slot][:], part_h[slot][:].bitcast(F32), ALU.subtract
                                        ).then_inc(sem["part_l_ready"], 1)

            def gather(e, id_sem, count):
                nc.gpsimd.tensor_copy(id_gather[:], tok_id[:, bass.ds(e, 1)]).then_inc(id_sem, 1)
                pool.wait_ge(sem["ident_ready"], 2)
                pool.wait_ge(id_sem, count)
                nc.gpsimd.indirect_dma_start(xg[:], None, n_scr, bass.IndirectOffsetOnAxis(ap=id_gather[:, 0:1], axis=0)
                                             ).then_inc(sem["gathered"], 16)

            def scatter(e, count):
                wait_past(pool, sem["scattered"], e * 16)
                pool.wait_ge(sem["y_ready"], count * 2)
                nc.gpsimd.tensor_copy(id_scatter[:], tok_id[:, bass.ds(e, 1)]).then_inc(sem["id2_ready"], 1)
                pool.wait_ge(sem["ident_ready"], 2)
                pool.wait_ge(sem["id2_ready"], count)
                nc.gpsimd.indirect_dma_start(x_scr, bass.IndirectOffsetOnAxis(ap=id_scatter[:, 0:1], axis=0), y_out[:],
                                             None, compute_op=ALU.add).then_inc(sem["scattered"], 16)

            pool.wait_ge(sem["chosen_ready"], 2)
            for i in range(2):
                pool.wait_ge(x2_stored[i], PER_SLOT)
                pool.wait_ge(n_stored[i], PER_SLOT)
            gather(0, sem["first_id_ready"], 1)
            pool.wait_ge(sem["gathered"], 16)
            pool.wait_ge(sem["xgT_h_ready"], 1)
            gather(1, sem["id_ready"], 1)
            scatter(0, 1)
            with pool.Fori(1, E - 1) as e:
                pool.wait_ge(sem["gathered"], (e + 1) * 16)
                pool.wait_ge(sem["xgT_h_ready"], e + 1)
                gather(e + 1, sem["id_ready"], e + 1)
                scatter(e, e + 1)
            scatter(E - 1, E)
            pool.wait_ge(sem["scattered"], 16 * E)
            pool.wait_ge(sem["y_stored"], 32 * NB)
            pool.wait_ge(sem["mod_stored"], 16 * N_ADA2)

        @block.scalar
        def _(act):
            def copy(dst, src):
                return nc.scalar.activation(dst, src, ACT.Identity)

            act.wait_ge(sem["vec_ready"], 1)
            nc.scalar.activation(silu_c[:].rearrange("p b k -> p (b k)"), vec1[:, V_C:V_END], ACT.Silu).then_inc(sem["silu_ready"], 1)
            act.wait_ge(sem["softplus_step"], 2)
            nc.scalar.activation(soft[:, 2, :], soft[:, 1, :], ACT.Exp, scale=-1.0).then_inc(sem["exp_done"], 1)
            for t in range(NT + NCT):
                if t == 4:
                    act.wait_ge(sem["win_loaded"], 64)
                    copy(win_h[0][:], win_raw[:])
                    copy(gatew_h[0][:], gate_raw[:]).then_inc(sem["win_h_ready"], 1)
                act.wait_ge(x_loaded[t], 16)
                nc.scalar.activation(junk[:], xbuf[:, t, :], ACT.Square, accum_out=stat[:, 0, t:t + 1]).then_inc(sem["squares_done"], 1)
                act.wait_ge(sem["squares_done"], t + 1)
                if t % 4 == 3 or t == NT + NCT - 1:
                    lo = t - t % 4
                    act.wait_ge(sem["ident_ready"], 2)
                    nc.scalar.activation(stat[:, 1, lo:t + 1], stat[:, 0, lo:t + 1], ACT.Sqrt, scale=1.0 / D,
                                         bias=eps[:]).then_inc(sem["rms_done"], 1)
            act.wait_ge(sem["mod_col_ready"], 3)
            for n, (g, k) in enumerate(groups):
                lo, w = SEGS[g]
                b = 1 if g == 2 else 0
                act.wait_ge(sem["x_turned"], n + 1)
                if n >= NH:
                    act.wait_ge(sem["hT_l_ready"], n - NH + 1)
                nc.scalar.activation(hf[:, n % NH, 0:w], bank(4 + n % 4)[:, 0:w], ACT.Identity, scale=scale1[:, b, k:k + 1],
                                     bias=mod_col[:, b, k:k + 1]).then_inc(sem["hf_ready"], 1)

            def split_win(n, slot):
                act.wait_ge(sem["win_loaded"], n * 64 + 64)
                wait_past(act, sem["gate_done"], (n - 1) * 12)
                copy(win_h[slot][:], win_raw[:])
                copy(gatew_h[slot][:], gate_raw[:]).then_inc(sem["win_h_ready"], 1)

            def mixer_block(n, slot, first=False, last=False):
                wait_past(act, sem["v_done"], n * 2)
                wait_past(act, sem["u_l_ready"], n)
                act.wait_ge(sem["u_done"], n + 1)
                nc.scalar.activation(u[:], pu[:, 0:LEN], ACT.Identity, scale=block_col[slot][:, 5 + CENTRE:6 + CENTRE],
                                     bias=block_col[slot][:, 0:1]).then_inc(sem["conv_init"], 1)
                if not first:
                    roots(n - 1)
                act.wait_ge(sem["conv_done"], (n + 1) * 6)
                wait_past(act, sem["gate_done"], n * 12)
                copy(u_h[:], u[:]).then_inc(sem["u_h_ready"], 1)
                if not last:
                    split_win(n + 1, 1 - slot)
                wait_past(act, sem["b_done"], n * 2)
                for m in range(4):
                    d, is_i = divmod(m, 2)
                    col = block_col[slot][:, 1 + 2 * is_i + d:2 + 2 * is_i + d]
                    for g, (lo, w) in enumerate(SEGS):
                        act.wait_ge(sem["gate_done"], n * 12 + 3 * m + g + 1)
                        nc.scalar.activation((i_d if is_i else r_d)[d][:, lo:lo + w], bank(5 + g)[:, 0:w], ACT.Sigmoid,
                                             bias=col).then_inc(sem["sig_done"], 1)
                if not first:
                    high_y(n - 1)
                wait_past(act, sem["y_done"], n)
                for d in range(2):
                    act.wait_ge(sem["sig_done"], n * 12 + 6 * d + 3)
                    nc.scalar.activation(a_d[d][:], r_d[d][:], ACT.Exp, scale=block_col[slot][:, 9 + d:10 + d]).then_inc(sem["a_done"], 1)
                    nc.scalar.activation(t_d[d][:], r_d[d][:], ACT.Tanh, scale=block_col[slot][:, 11 + d:12 + d]).then_inc(sem["t_done"], 1)
                act.wait_ge(sem["g_done"], n + 1)
                wait_past(act, sem["y_l_ready"], n)
                nc.scalar.activation(y[:], psum[:, 3:5, :].rearrange("p b f -> p (b f)"),
                                     ACT.Gelu_apprx_tanh).then_inc(sem["gelu_done"], 1)

            def roots(n):
                for d in range(2):
                    act.wait_ge(sem["w_done"], n * 2 + d + 1)
                    nc.scalar.activation(t_d[d][:], t_d[d][:], ACT.Sqrt).then_inc(sem["s_done"], 1)

            def high_y(n):
                act.wait_ge(sem["y_done"], n + 1)
                wait_past(act, sem["y_stored"], n * 32)
                copy(y_h[:], y[:]).then_inc(sem["y_h_ready"], 1)

            mixer_block(0, 0, first=True)
            mixer_block(1, 1)
            with act.Fori(1, NB // 2 - 1) as j:
                mixer_block(j * 2, 0)
                mixer_block(j * 2 + 1, 1)
            mixer_block(NB - 2, 0)
            mixer_block(NB - 1, 1, last=True)
            roots(NB - 1)

            high_y(NB - 1)

            def norm2(t, slot, j):
                act.wait_ge(sem["x2_ready"], t + 1)
                if j is not None:
                    act.wait_ge(n_stored[slot], j * 16)
                    act.wait_ge(sem["xn_turned"], t - 1)
                nc.scalar.activation(xn[slot][:], x2[slot][:], ACT.Square, accum_out=stat[:, 0, slot:slot + 1]).then_inc(sem["sq2_done"], 1)
                act.wait_ge(sem["sq2_done"], t + 1)
                nc.scalar.activation(stat[:, 1, slot:slot + 1], stat[:, 0, slot:slot + 1], ACT.Sqrt, scale=1.0 / D,
                                     bias=eps[:]).then_inc(sem["rms2_done"], 1)

            def modulate2(t):
                act.wait_ge(sem["xn_turned"], t + 1)
                wait_past(act, sem["logits_done"], t)
                for k in range(KD):
                    last = nc.scalar.activation(h2T[:, k, :], bank(4 + k // 4)[:, (k % 4) * P:(k % 4 + 1) * P], ACT.Identity,
                                                scale=scale2[:, k:k + 1], bias=shift2[:, k:k + 1])
                last.then_inc(sem["h2T_ready"], 1)

            act.wait_ge(sem["mod2_step"], 2)
            norm2(0, 0, None)
            norm2(1, 1, None)
            act.wait_ge(sem["y_stored"], 32 * NB)
            modulate2(0)
            with act.Fori(1, NT // 2) as j:
                for slot in range(2):
                    t = j * 2 + slot
                    norm2(t, slot, j)
                    modulate2(t - 1)
            modulate2(NT - 1)

            act.wait_ge(sem["soft_step"], 2)
            nc.scalar.activation(soft[:, 0:NT, 0:E], soft[:, 0:NT, 0:E], ACT.Exp).then_inc(sem["exp_done"], 1)

            def split(e, key):
                i = at[key]
                slot = i % NS
                uses = 0 if slot < 2 else 16
                act.wait_ge(raw_loaded[slot], e * (CH // NS * 16) + (i // NS) * 16 + uses)
                if not (isinstance(e, int) and e == 0 and i < 2 + NS):
                    act.wait_ge(sem["chunk_used"], e * CH + i - NS - 1)
                copy(part_h[slot][:], raw[slot][:]).then_inc(sem["part_h_ready"], 1)

            act.wait_ge(sem["gated_done"], 2 * NT)
            for key in order[2:2 + NS]:
                split(0, key)

            def hidden(e, f):
                act.wait_ge(sem["chunk_used"], gate_at(e, f))
                if not (isinstance(e, int) and e == 0 and f < 2):
                    act.wait_ge(sem["hid_ready"], e * NF + f - 1)
                nc.scalar.activation(act_g[f % 2][:], bank(2 * (f % 2)), ACT.Silu).then_inc(sem["silu_done"], 1)

            def turn_hidden(e, f):
                act.wait_ge(sem["hid_turned"], e * NF + f + 1)
                if not (isinstance(e, int) and e == 0 and f < 2):
                    act.wait_ge(sem["chunk_used"], down_at(*two_before(e, f)))
                copy(hidT_h[f % 2][:], bank(4 + f % 2)).then_inc(sem["hidT_h_ready"], 1)

            def expert(e, first=False):
                if not first:
                    split(e, ("d", 3, 0))
                    split(e, ("d", 3, 1))
                    turn_hidden(e - 1, 3)
                for k in range(KD):
                    if k % 4 == 0:
                        act.wait_ge(sem["xg_turned"], e * 2 + k // 4 + 1)
                    if k == 0:
                        wait_past(act, sem["xgT_l_ready"], e)
                    last = nc.scalar.activation(xgT[:, k, :], bank(k // 4)[:, (k % 4) * P:(k % 4 + 1) * P],
                                                ACT.Identity, scale=scale2[:, k:k + 1], bias=shift2[:, k:k + 1])
                    if k % 4 == 3:
                        last.then_inc(sem["xgT_ready"], 1)
                act.wait_ge(sem["xgT_ready"], e * 2 + 2)
                if not first:
                    act.wait_ge(sem["chunk_used"], up_at(e - 1, NF - 1))
                copy(xgT_h[:], xgT[:]).then_inc(sem["xgT_h_ready"], 1)
                for f in range(NF):
                    for key in (("g", f, 0), ("g", f, 1), ("u", f, 0), ("u", f, 1)):
                        if not (first and at[key] < 2 + NS):
                            split(e, key)
                    if f:
                        turn_hidden(e, f - 1)
                    hidden(e, f)
                    if f:
                        split(e, ("d", f - 1, 0))
                        split(e, ("d", f - 1, 1))

            expert(0, first=True)
            with act.Fori(1, E) as e:
                expert(e)
            split(E, ("d", 3, 0))
            split(E, ("d", 3, 1))
            turn_hidden(E - 1, 3)

            act.wait_ge(sem["chunk_used"], E * CH)
            for t in range(NT):
                act.wait_ge(fin_loaded[t], 16)
                nc.scalar.activation(fin_junk[:], fin_in[:, t, :], ACT.Square, accum_out=stat[:, 0, t:t + 1]).then_inc(sem["fin_sq"], 1)
                act.wait_ge(sem["fin_sq"], t + 1)
                nc.scalar.activation(stat[:, 1, t:t + 1], stat[:, 0, t:t + 1], ACT.Sqrt, scale=1.0 / D,
                                     bias=eps[:]).then_inc(sem["fin_rms"], 1)

        @block.vector
        def _(dve):
            v = nc.vector

            dve.wait_ge(sem["vec_turned"], 1)
            v.tensor_copy(vec1[:, 0:V_END], bank(3)[:, 0:V_END]).then_inc(sem["vec_ready"], 1)
            v.tensor_copy(taps[:], bank(3)[:, P:P + TAPS * NB]).then_inc(sem["vec_ready"], 1)
            count = [0]

            def step(ins):
                count[0] += 1
                ins.then_inc(sem["softplus_step"], 1)
                dve.wait_ge(sem["softplus_step"], count[0])

            lam = vec1[:, V_LAM:V_LAM + 2 * NB]
            dve.wait_ge(sem["vec_ready"], 2)
            step(v.tensor_scalar(soft[:, 0, :], lam, -1.0, None, ALU.mult))
            step(v.tensor_tensor(soft[:, 1, :], soft[:, 0, :], lam, ALU.max))
            dve.wait_ge(sem["exp_done"], 1)
            step(v.tensor_scalar(soft[:, 3, :], soft[:, 2, :], 2.0, None, ALU.add))
            step(v.reciprocal(soft[:, 4, :], soft[:, 3, :]))
            step(v.tensor_tensor(soft[:, 3, :], soft[:, 2, :], soft[:, 4, :], ALU.mult))
            step(v.tensor_tensor(soft[:, 4, :], soft[:, 3, :], soft[:, 3, :], ALU.mult))
            step(v.tensor_scalar(soft[:, 5, :], soft[:, 4, :], 2.0 / 17, 2.0 / 15, ALU.mult, ALU.add))
            for m in (13, 11, 9, 7, 5, 3, 1):
                step(v.tensor_tensor(soft[:, 5, :], soft[:, 5, :], soft[:, 4, :], ALU.mult))
                step(v.tensor_scalar(soft[:, 5, :], soft[:, 5, :], 2.0 / m, None, ALU.add))
            step(v.tensor_tensor(soft[:, 5, :], soft[:, 5, :], soft[:, 3, :], ALU.mult))
            step(v.scalar_tensor_tensor(soft[:, 6, :], soft[:, 0, :], 0.0, soft[:, 5, :], ALU.max, ALU.add))
            step(v.tensor_scalar(rate[:, 0, :], soft[:, 6, :], -RG_C, None, ALU.mult))
            step(v.tensor_scalar(rate[:, 1, :], soft[:, 6, :], RG_C, None, ALU.mult))

            def mod_chunk(i):
                dve.wait_ge(sem["mod_rows_done"], i + 1)
                if i >= 2:
                    dve.wait_ge(sem["mod_turned"], i - 1)
                v.tensor_copy(mod_rows[:, i % 2, :], bank(i % 2)[0:2, :]).then_inc(sem["mod_rows_ready"], 1)

            def normed(lo, hi, part):
                dve.wait_ge(sem["rms_done"], part + 1)
                v.reciprocal(stat[:, 0, lo:hi], stat[:, 1, lo:hi]).then_inc(sem["rstd_ready"], 1)
                dve.wait_ge(sem["rstd_ready"], part + 1)
                for t in range(lo, hi):
                    v.tensor_scalar(xbuf[:, t, :], xbuf[:, t, :], stat[:, 0, t:t + 1], None, ALU.mult).then_inc(sem["xn_ready"], 1)

            def split_win(n, slot):
                dve.wait_ge(sem["win_h_ready"], n + 1)
                for lo, hi, src in ((0, 5, vec1[:, V_CB:V_CB + 5 * NB]), (5, 9, taps[:]), (9, 13, rate[:].rearrange("p s c -> p (s c)"))):
                    v.tensor_scalar(block_col[slot][:, lo:hi].rearrange("p (a o) -> p a o", o=1),
                                    src.rearrange("p (a n) -> p a n", n=NB)[:, :, bass.ds(n, 1)], 1.0, None, ALU.mult)
                v.tensor_tensor(win_l[slot][:], win_raw[:], win_h[slot][:].bitcast(F32), ALU.subtract)
                v.tensor_tensor(gatew_l[slot][:], gate_raw[:], gatew_h[slot][:].bitcast(F32),
                                ALU.subtract).then_inc(sem["win_l_ready"], 1)

            mod_chunk(0)
            normed(0, 4, 0)
            mod_chunk(1)
            split_win(0, 0)
            mod_chunk(2)
            mod_chunk(3)
            dve.wait_ge(sem["mod_turned"], N_ADA1)
            v.tensor_tensor(mod_col[:].rearrange("p b m -> p m b"), bank(2)[:, 0:32].rearrange("p (m b) -> p m b", b=2),
                            vec1[:, V_ADA:V_ADA + 16].rearrange("p (m o) -> p m o", o=1).broadcast_to((P, 16, 2)),
                            ALU.add).then_inc(sem["mod_col_ready"], 1)
            dve.wait_ge(sem["mod_col_ready"], 1)
            for b in range(2):
                v.scalar_tensor_tensor(scale1[:, b, :], mod_col[:, b, KD:2 * KD], 1.0, vec1[:, V_NM:V_NM + KD],
                                       ALU.add, ALU.mult).then_inc(sem["mod_col_ready"], 1)
            normed(4, 8, 1)
            dve.wait_ge(sem["mod_col_ready"], 3)
            for n, (g, k) in enumerate(groups):
                lo, w = SEGS[g]
                dve.wait_ge(sem["hT_h_ready"], n + 1)
                v.tensor_tensor(hT_l[:, k, lo:lo + w], hf[:, n % NH, 0:w], hT_h[:, k, lo:lo + w].bitcast(F32),
                                ALU.subtract).then_inc(sem["hT_l_ready"], 1)
                if n == 3:
                    normed(8, 10, 2)

            def mixer_block(n, slot, ada, first=False, last=False):
                lat, con = (u[:, 0:SEQ].rearrange("p (r w) -> p r w", w=GRID_W), u[:, SEQ:LEN])
                z_lat, z_con = (pu[:, 0:SEQ].rearrange("p (r w) -> p r w", w=GRID_W), pu[:, SEQ:LEN])
                dve.wait_ge(sem["conv_init"], n + 1)
                for i, j in enumerate([0, 1, 3]):
                    off = j - CENTRE
                    a, b = max(0, -off), max(0, off)
                    col = block_col[slot][:, 5 + j:6 + j]
                    if i:
                        dve.wait_ge(sem["conv_done"], n * 6 + 2 * i)
                    v.scalar_tensor_tensor(lat[:, :, a:GRID_W - b], z_lat[:, :, b:GRID_W - a], col, lat[:, :, a:GRID_W - b],
                                           ALU.mult, ALU.add).then_inc(sem["conv_done"], 1)
                    v.scalar_tensor_tensor(con[:, a:CTX - b], z_con[:, b:CTX - a], col, con[:, a:CTX - b],
                                           ALU.mult, ALU.add).then_inc(sem["conv_done"], 1)
                dve.wait_ge(sem["u_h_ready"], n + 1)
                v.tensor_tensor(u_l[:], u[:], u_h[:].bitcast(F32), ALU.subtract).then_inc(sem["u_l_ready"], 1)
                if ada:
                    dve.wait_ge(sem["ada_done"], n)
                    dve.wait_ge(sem["bias_loaded"], n * 16)
                    v.tensor_tensor(mod_out[:], bank(7)[0:1, :], mod_out[:], ALU.add).then_inc(sem["ada_out"], 1)
                if not first:
                    scan_inputs(n - 1)
                if not last:
                    split_win(n + 1, 1 - slot)
                if not first:
                    scans(n - 1)
                    low_y(n - 1)
                if last:
                    wo_low(0)
                    wo_low(1)
                for d in range(2):
                    dve.wait_ge(sem["t_done"], n * 2 + d + 1)
                    v.tensor_tensor(r_d[d][:], a_d[d][:], a_d[d][:], ALU.mult).then_inc(sem["q_done"], 1)
                    dve.wait_ge(sem["q_done"], n * 2 + d + 1)
                    v.scalar_tensor_tensor(t_d[d][:], r_d[d][:], 1.0, t_d[d][:], ALU.add, ALU.mult).then_inc(sem["w_done"], 1)

            def wo_low(i):
                dve.wait_ge(sem["wo_h_ready"], i + 1)
                cols = slice(2 * i * D, (2 * i + 2) * D)
                v.tensor_tensor(act_l[:, cols], wo_raw[i][:].rearrange("p k f -> p (k f)"), act_h[:, cols].bitcast(F32),
                                ALU.subtract).then_inc(sem["wo_l_dve"], 1)

            def scan_inputs(n):
                for d in range(2):
                    dve.wait_ge(sem["s_done"], n * 2 + d + 1)
                    dve.wait_ge(sem["v_done"], n * 2 + d + 1)
                    v.tensor_tensor(t_d[d][:], t_d[d][:], i_d[d][:], ALU.mult).then_inc(sem["b_done"], 1)

            def scans(n):
                for d in range(2):
                    dve.wait_ge(sem["b_done"], n * 2 + d + 1)
                    h = t_d[d]
                    flip = (lambda ap: ap[:, ::-1]) if d else (lambda ap: ap)
                    v.tensor_tensor_scan(flip(h[:, SEQ:LEN]), flip(a_d[d][:, SEQ:LEN]), flip(t_d[d][:, SEQ:LEN]), 0.0,
                                         ALU.mult, ALU.add).then_inc(sem["scan_ctx"], 1)
                for d in range(2):
                    h = t_d[d]
                    flip = (lambda ap: ap[:, ::-1]) if d else (lambda ap: ap)
                    end = h[:, SEQ:SEQ + 1] if d else h[:, LEN - 1:LEN]
                    dve.wait_ge(sem["scan_ctx"], n * 2 + d + 1)
                    v.tensor_tensor_scan(flip(h[:, 0:SEQ]), flip(a_d[d][:, 0:SEQ]), flip(t_d[d][:, 0:SEQ]), end,
                                         ALU.mult, ALU.add).then_inc(sem["scan_done"], 1)
                dve.wait_ge(sem["scan_done"], n * 2 + 2)
                v.tensor_tensor(t_d[0][:, 0:SEQ], t_d[0][:, 0:SEQ], t_d[1][:, 0:SEQ], ALU.add).then_inc(sem["y_sum"], 1)
                dve.wait_ge(sem["y_sum"], n + 1)
                dve.wait_ge(sem["gelu_done"], n + 1)
                v.tensor_tensor(y[:], y[:], t_d[0][:, 0:SEQ], ALU.mult).then_inc(sem["y_done"], 1)

            def low_y(n):
                dve.wait_ge(sem["y_h_ready"], n + 1)
                v.tensor_tensor(y_l[:], y[:], y_h[:].bitcast(F32), ALU.subtract).then_inc(sem["y_l_ready"], 1)

            mixer_block(0, 0, False, first=True)
            mixer_block(1, 1, True)
            with dve.Fori(1, NB // 2 - 1) as j:
                mixer_block(j * 2, 0, True)
                mixer_block(j * 2 + 1, 1, True)
            mixer_block(NB - 2, 0, True)
            mixer_block(NB - 1, 1, False, last=True)
            wo_low(2)
            scan_inputs(NB - 1)
            scans(NB - 1)
            low_y(NB - 1)

            dve.wait_ge(sem["rows3_turned"], 1)
            v.tensor_copy(shift2[:], bank(7)[:, 0:KD]).then_inc(sem["mod2_step"], 1)
            v.scalar_tensor_tensor(scale2[:], bank(7)[:, KD:2 * KD], 1.0, vec1[:, V_NF:V_NF + KD], ALU.add, ALU.mult).then_inc(sem["mod2_step"], 1)

            def residual(t, slot, j):
                for half in range(2):
                    dve.wait_ge(sem["proj_done"], t * 2 + half + 1)
                    if j is not None:
                        dve.wait_ge(x2_stored[slot], j * 16)
                    cols = slice(half * HALF, (half + 1) * HALF)
                    v.tensor_tensor(x2[slot][:, cols], bank(2 * slot + half), gate2_row[:, cols], ALU.mult).then_inc(sem["gated_done"], 1)
                dve.wait_ge(sem["gated_done"], t * 2 + 2)
                v.tensor_tensor(x2[slot][:], x2[slot][:], xt[slot][:], ALU.add).then_inc(sem["x2_ready"], 1)

            def scale_rows(t, slot):
                dve.wait_ge(sem["rms2_done"], t + 1)
                v.reciprocal(stat[:, 0, slot:slot + 1], stat[:, 1, slot:slot + 1]).then_inc(sem["rstd2_ready"], 1)
                dve.wait_ge(sem["rstd2_ready"], t + 1)
                v.tensor_scalar(xn[slot][:], x2[slot][:], stat[:, 0, slot:slot + 1], None, ALU.mult).then_inc(sem["xn2_ready"], 1)

            dve.wait_ge(sem["late_loaded"], 48)
            for t in range(2):
                dve.wait_ge([sem["xt_loaded_a"], sem["xt_loaded_b"]][t], 16)
                residual(t, t, None)
                scale_rows(t, t)
            with dve.Fori(1, NT // 2) as j:
                for slot in range(2):
                    t = j * 2 + slot
                    dve.wait_ge([sem["xt_loaded_a"], sem["xt_loaded_b"]][slot], j * 16 + 16)
                    residual(t, slot, j)
                    scale_rows(t, slot)

            logits = bank(6)[:, 0:NT * E].rearrange("p (t e) -> p t e", e=E)
            ex = soft[:, 0:NT, 0:E]
            col = lambda i: stat[:, i, 0:NT]
            wide = lambda i: col(i).rearrange("p (t o) -> p t o", o=1).broadcast_to((P, NT, E))
            dve.wait_ge(sem["logits_done"], NT)
            v.tensor_reduce(col(0), logits, AX.X, ALU.max).then_inc(sem["soft_step"], 1)
            dve.wait_ge(sem["soft_step"], 1)
            v.tensor_tensor(ex, logits, wide(0), ALU.subtract).then_inc(sem["soft_step"], 1)
            dve.wait_ge(sem["exp_done"], 2)
            v.tensor_reduce(col(0), ex, AX.X, ALU.add).then_inc(sem["soft_step"], 1)
            dve.wait_ge(sem["soft_step"], 3)
            v.reciprocal(col(1), col(0)).then_inc(sem["soft_step"], 1)
            dve.wait_ge(sem["soft_step"], 4)
            v.tensor_tensor(ex, ex, wide(1), ALU.mult).then_inc(sem["soft_step"], 1)

            dve.wait_ge(sem["aff_turned"], 1)
            for i in range(2):
                dve.wait_ge(x2_stored[i], PER_SLOT)
            v.tensor_copy(aff_row[0][:], psum[0:E, 0:2, :].rearrange("p b f -> p (b f)")).then_inc(sem["aff_row_ready"], 1)
            dve.wait_ge(sem["aff_row_ready"], 1)
            for r in range(CAP // 8):
                src, dst = aff_row[r % 2], aff_row[1 - r % 2]
                best = top_val[:, 8 * r:8 * r + 8]
                v.max(best, src[:]).then_inc(sem["top_step"], 1)
                dve.wait_ge(sem["top_step"], 2 * r + 1)
                v.max_index(top_id[:, 8 * r:8 * r + 8], best, src[:])
                v.match_replace(dst[:], best, src[:], -1.0).then_inc(sem["top_step"], 1)
                dve.wait_ge(sem["top_step"], 2 * r + 2)
            v.tensor_copy(top_idf[:], top_id[:]).then_inc(sem["top_step"], 1)
            dve.wait_ge(sem["top_turned"], 1)
            v.tensor_copy(tok_id[:], bank(2)[:, 0:E]).then_inc(sem["chosen_ready"], 1)
            v.tensor_copy(gate_v[:], bank(2)[:, E:2 * E]).then_inc(sem["chosen_ready"], 1)
            dve.wait_ge(sem["chosen_ready"], 2)
            dve.wait_ge(sem["gate5_loaded"], 16)

            def split(e, key):
                i = at[key]
                slot = i % NS
                dve.wait_ge(sem["part_h_ready"], e * CH + i - 1)
                v.tensor_tensor(part_l[slot][:], raw[slot][:], part_h[slot][:].bitcast(F32), ALU.subtract).then_inc(sem["part_l_ready"], 1)

            def gate_up(e, f):
                dve.wait_ge(sem["silu_done"], e * NF + f + 1)
                dve.wait_ge(sem["chunk_used"], up_at(e, f))
                if not (isinstance(e, int) and e == 0 and f < 2):
                    dve.wait_ge(sem["hid_turned"], e * NF + f - 1)
                v.tensor_tensor(hid[f % 2][:], act_g[f % 2][:], bank(2 * (f % 2) + 1), ALU.mult).then_inc(sem["hid_ready"], 1)

            def turn_hidden(e, f):
                dve.wait_ge(sem["hidT_h_ready"], e * NF + f + 1)
                v.tensor_tensor(hidT_l[f % 2][:], bank(4 + f % 2).rearrange("p (k t) -> p k t", t=P), hidT_h[f % 2][:].bitcast(F32),
                                ALU.subtract).then_inc(sem["hidT_l_ready"], 1)

            def expert_out(e):
                dve.wait_ge(sem["chunk_used"], down_at(e, NF - 1))
                wait_past(dve, sem["scattered"], e * 16)
                for half in range(2):
                    cols = slice(half * HALF, (half + 1) * HALF)
                    v.scalar_tensor_tensor(y_out[:, cols], bank(6 + half), gate_v[:, bass.ds(e, 1)], gate5_row[:, cols],
                                           ALU.mult, ALU.mult).then_inc(sem["y_ready"], 1)

            def expert(e, first=False):
                if not first:
                    split(e, ("d", 3, 0))
                    split(e, ("d", 3, 1))
                    turn_hidden(e - 1, 3)
                dve.wait_ge(sem["xgT_h_ready"], e + 1)
                v.tensor_tensor(xgT_l[:], xgT[:], xgT_h[:].bitcast(F32), ALU.subtract).then_inc(sem["xgT_l_ready"], 1)
                for f in range(NF):
                    for key in (("g", f, 0), ("g", f, 1), ("u", f, 0), ("u", f, 1)):
                        if not (first and at[key] < 2 + NS):
                            split(e, key)
                    if f:
                        turn_hidden(e, f - 1)
                        split(e, ("d", f - 1, 0))
                        split(e, ("d", f - 1, 1))
                    elif not first:
                        expert_out(e - 1)
                    gate_up(e, f)

            expert(0, first=True)
            with dve.Fori(1, E) as e:
                expert(e)
            split(E, ("d", 3, 0))
            split(E, ("d", 3, 1))
            turn_hidden(E - 1, 3)
            expert_out(E - 1)

            dve.wait_ge(sem["fin_g_loaded"], 16)
            for t in range(NT):
                dve.wait_ge(sem["fin_rms"], t + 1)
                v.reciprocal(stat[:, 0, t:t + 1], stat[:, 1, t:t + 1]).then_inc(sem["fin_rstd"], 1)
                dve.wait_ge(sem["fin_rstd"], t + 1)
                v.scalar_tensor_tensor(fin_out[:, t, :], fin_in[:, t, :], stat[:, 0, t:t + 1], fin_g[:], ALU.mult, ALU.mult
                                       ).then_inc(sem["fin_ready"], 1)

        @block.tensor
        def _(pe):
            mm = nc.tensor.matmul

            def three(out_ap, pairs):
                for i, ((xh, xl), (wh, wl)) in enumerate(pairs):
                    mm(out_ap, xh, wh, start=(i == 0), stop=False)
                    mm(out_ap, xl, wh, start=False, stop=False)
                    last = mm(out_ap, xh, wl, start=False, stop=(i == len(pairs) - 1))
                return last

            pe.wait_ge(sem["small_loaded"], 16 * len(small))
            pe.wait_ge(sem["ident_ready"], 2)
            nc.tensor.transpose(bank(3)[:, 0:V_END], rows1[0:V_END, :], ident[0:V_END, 0:V_END])
            nc.tensor.transpose(bank(3)[:, P:P + TAPS * NB], rows2[0:TAPS * NB, :], ident[0:TAPS * NB, 0:TAPS * NB]
                                ).then_inc(sem["vec_turned"], 1)

            def mod_product(i):
                if i == 0:
                    pe.wait_ge(sem["silu_ready"], 1)
                pe.wait_ge(ada_loaded[i], 16)
                if i >= 2:
                    pe.wait_ge(sem["mod_rows_ready"], i - 1)
                for k in range(KD):
                    last = mm(bank(i % 2)[0:2, :], silu_c[:, :, k], ada1[i][:, k, :], start=(k == 0), stop=(k == KD - 1))
                last.then_inc(sem["mod_rows_done"], 1)

            def mod_turn(i):
                pe.wait_ge(sem["mod_rows_ready"], i + 1)
                for q in range(4):
                    last = nc.tensor.transpose(bank(2)[:, 2 * (4 * i + q):2 * (4 * i + q) + 2],
                                               mod_rows[:, i % 2, q * P:(q + 1) * P], ident[0:2, 0:2])
                last.then_inc(sem["mod_turned"], 1)

            for i in range(N_ADA1):
                mod_product(i)
                if i:
                    mod_turn(i - 1)
            mod_turn(N_ADA1 - 1)
            for n, (g, k) in enumerate(groups):
                tiles = seg_tiles[g]
                pe.wait_ge(sem["xn_ready"], tiles[-1] + 1)
                if n >= 4:
                    pe.wait_ge(sem["hf_ready"], n - 3)
                for i, t in enumerate(tiles):
                    last = nc.tensor.transpose(bank(4 + n % 4)[:, i * P:(i + 1) * P], xbuf[:, t, k * P:(k + 1) * P], ident[:])
                last.then_inc(sem["x_turned"], 1)
                if g:
                    lo, w = SEGS[g - 1]
                    pe.wait_ge(sem["win_l_ready"], 1)
                    pe.wait_ge(sem["hT_l_ready"], n - KD + 1)
                    wh, wl = win_h[0][:, k, P:2 * P], win_l[0][:, k, P:2 * P]
                    mm(pu[:, lo:lo + w], wh, hT_h[:, k, lo:lo + w], start=(k == 0), stop=False)
                    mm(pu[:, lo:lo + w], wl, hT_h[:, k, lo:lo + w], start=False, stop=False)
                    mm(pu[:, lo:lo + w], wh, hT_l[:, k, lo:lo + w], start=False, stop=(k == KD - 1))

            pe.wait_ge(sem["hf_ready"], len(groups))
            pe.wait_ge(sem["mod_col_ready"], 1)
            pe.wait_ge(sem["hT_l_ready"], len(groups))

            def mixer_block(n, slot, ada, segs_done=0):
                wh, wl, gh, gl = win_h[slot], win_l[slot], gatew_h[slot], gatew_l[slot]
                project = lambda out_ap, c0, lo, w: three(out_ap, [
                    ((wh[:, k, c0:c0 + P], wl[:, k, c0:c0 + P]), (hT_h[:, k, lo:lo + w], hT_l[:, k, lo:lo + w])) for k in range(KD)])
                pe.wait_ge(sem["win_l_ready"], n + 1)
                wait_past(pe, sem["conv_done"], n * 6)
                for lo, w in SEGS[segs_done:]:
                    last = project(pu[:, lo:lo + w], P, lo, w)
                last.then_inc(sem["u_done"], 1)
                if ada:
                    pe.wait_ge(sem["piece_used"], n * KD)
                    pe.wait_ge(sem["sig_done"], n * 12)
                    mm(bank(7)[0:1, :], ones[:], ada_sum[:], start=True, stop=True).then_inc(sem["ada_done"], 1)
                wait_past(pe, sem["gelu_done"], n)
                for half in range(2):
                    last = project(bank(3 + half), 0, half * HALF, HALF)
                last.then_inc(sem["g_done"], 1)
                pe.wait_ge(sem["u_l_ready"], n + 1)
                if ada:
                    pe.wait_ge(sem["ada_out"], n)
                for m in range(4):
                    d, is_i = divmod(m, 2)
                    q = 2 * is_i + d
                    for g, (lo, w) in enumerate(SEGS):
                        if m == 0:
                            wait_past(pe, sem["sig_done"], n * 12)
                        else:
                            pe.wait_ge(sem["sig_done"], n * 12 + 3 * (m - 1) + g + 1)
                        three(bank(5 + g)[:, 0:w], [((gh[:, q, :], gl[:, q, :]), (u_h[:, lo:lo + w], u_l[:, lo:lo + w]))]
                              ).then_inc(sem["gate_done"], 1)

            mixer_block(0, 0, False, segs_done=2)
            mixer_block(1, 1, True)
            with pe.Fori(1, NB // 2 - 1) as j:
                mixer_block(j * 2, 0, True)
                mixer_block(j * 2 + 1, 1, True)
            mixer_block(NB - 2, 0, True)
            mixer_block(NB - 1, 1, False)

            def project_out(t, slot, uses, first):
                pe.wait_ge([sem["yt_loaded_a"], sem["yt_loaded_b"]][slot], uses)
                for half in range(2):
                    if not first:
                        pe.wait_ge(sem["gated_done"], (t - 1) * 2)
                    out_ap, cols = bank(2 * slot + half), slice(half * HALF, (half + 1) * HALF)
                    for n in range(NB):
                        yh, yl = yt_h[slot][:, n, :], yt_l[slot][:, n, :]
                        if first and n == NB - 1:
                            pe.wait_ge(sem["y_l_ready"], NB)
                            yh, yl = y_h[:, t * P:(t + 1) * P], y_l[:, t * P:(t + 1) * P]
                        mm(out_ap, yh, wo_h[:, n, cols], start=(n == 0), stop=False)
                        mm(out_ap, yl, wo_h[:, n, cols], start=False, stop=False)
                        last = mm(out_ap, yh, wo_l[:, n, cols], start=False, stop=(n == NB - 1))
                    last.then_inc(sem["proj_done"], 1)

            def turn_tile(t, slot):
                pe.wait_ge(sem["xn2_ready"], t + 1)
                wait_past(pe, sem["h2T_ready"], t)
                for k in range(KD):
                    last = nc.tensor.transpose(bank(4 + k // 4)[:, (k % 4) * P:(k % 4 + 1) * P], xn[slot][:, k * P:(k + 1) * P], ident[:])
                last.then_inc(sem["xn_turned"], 1)

            def route(t):
                pe.wait_ge(sem["h2T_ready"], t + 1)
                for k in range(KD):
                    last = mm(bank(6)[:, bass.ds(t * E, E)], h2T[:, k, :], router[:, k, :], start=(k == 0), stop=(k == KD - 1))
                last.then_inc(sem["logits_done"], 1)

            pe.wait_ge(sem["wo_l_dve"], WO_DVE)
            pe.wait_ge(sem["wo_l_pool"], NB // 2 - WO_DVE)
            pe.wait_ge(sem["conv_done"], 6 * NB)
            project_out(0, 0, 32, True)
            pe.wait_ge(sem["late_loaded"], 48)
            pe.wait_ge(sem["sig_done"], 12 * NB)
            pe.wait_ge(sem["gelu_done"], NB)
            nc.tensor.transpose(bank(7)[:, 0:2 * KD], rows3[:], ident[0:2 * KD, 0:2 * KD]).then_inc(sem["rows3_turned"], 1)
            project_out(1, 1, 32, True)
            turn_tile(0, 0)
            with pe.Fori(1, NT // 2) as j:
                for slot in range(2):
                    t = j * 2 + slot
                    project_out(t, slot, j * 32 + 32, False)
                    route(t - 2)
                    turn_tile(t - 1, 1 - slot)
            route(NT - 2)
            turn_tile(NT - 1, 1)
            route(NT - 1)

            pe.wait_ge(sem["soft_step"], 5)
            for t in range(NT):
                last = nc.tensor.transpose(psum[0:E, t // 4, (t % 4) * P:(t % 4 + 1) * P], soft[:, t, 0:E], ident[:])
            last.then_inc(sem["aff_turned"], 1)
            pe.wait_ge(sem["top_step"], 2 * (CAP // 8) + 1)
            nc.tensor.transpose(bank(2)[:, 0:E], top_idf[:], ident[0:E, 0:E])
            nc.tensor.transpose(bank(2)[:, E:2 * E], top_val[:], ident[0:E, 0:E]).then_inc(sem["top_turned"], 1)

            def weights(kind, slot):
                n = 2 if kind == "d" else 4
                r = lambda ap: ap[:].rearrange("p (k f) -> p k f", k=n)
                return r(part_h[slot]), r(part_l[slot])

            def in_product(e, kind, f):
                dst = bank(2 * (f % 2) + (kind == "u"))
                if not (isinstance(e, int) and e == 0 and f < 2):
                    pe.wait_ge(sem["hid_ready"], e * NF + f - 1)
                for half in range(2):
                    key = (kind, f, half)
                    wh, wl = weights(kind, at[key] % NS)
                    pe.wait_ge(sem["part_l_ready"], used(e, key))
                    for k in range(4):
                        kk = 4 * half + k
                        mm(dst, xgT_h[:, kk, :], wh[:, k, :], start=(kk == 0), stop=False)
                        mm(dst, xgT_l[:, kk, :], wh[:, k, :], start=False, stop=False)
                        last = mm(dst, xgT_h[:, kk, :], wl[:, k, :], start=False, stop=(kk == KD - 1))
                    if half == 0:
                        last.then_inc(sem["chunk_used"], 1)
                last.then_inc(sem["chunk_used"], 1)

            def turn_hidden(e, f):
                pe.wait_ge(sem["hid_ready"], e * NF + f + 1)
                for k in range(4):
                    last = nc.tensor.transpose(bank(4 + f % 2)[:, k * P:(k + 1) * P], hid[f % 2][:, k * P:(k + 1) * P], ident[:])
                last.then_inc(sem["hid_turned"], 1)

            def down_product(e, f, e_at):
                pe.wait_ge(sem["hidT_l_ready"], e * NF + f + 1)
                if f == 0:
                    wait_past(pe, sem["y_ready"], e * 2)
                for half in range(2):
                    key = ("d", f, half)
                    wh, wl = weights("d", at[key] % NS)
                    pe.wait_ge(sem["part_l_ready"], used(e_at, key))
                    for k in range(2):
                        kk = 2 * half + k
                        for n in range(2):
                            cols = slice(n * HALF, (n + 1) * HALF)
                            first, final = f == 0 and kk == 0, f == NF - 1 and kk == 3
                            mm(bank(6 + n), hidT_h[f % 2][:, kk, :], wh[:, k, cols], start=first, stop=False)
                            mm(bank(6 + n), hidT_l[f % 2][:, kk, :], wh[:, k, cols], start=False, stop=False)
                            last = mm(bank(6 + n), hidT_h[f % 2][:, kk, :], wl[:, k, cols], start=False, stop=final)
                    if half == 0:
                        last.then_inc(sem["chunk_used"], 1)
                last.then_inc(sem["chunk_used"], 1)

            def turn_rows(e, first):
                pe.wait_ge(sem["gathered"], e * 16 + 16)
                for half in range(2):
                    if not first and half == 0:
                        pe.wait_ge(sem["hid_ready"], e * NF - 1)
                    for k in range(4):
                        kk = 4 * half + k
                        last = nc.tensor.transpose(bank(half)[:, k * P:(k + 1) * P], xg[:, kk * P:(kk + 1) * P], ident[:])
                    last.then_inc(sem["xg_turned"], 1)

            def expert(e, first=False):
                if not first:
                    turn_hidden(e - 1, 3)
                turn_rows(e, first)
                if not first:
                    down_product(e - 1, 3, e)
                pe.wait_ge(sem["xgT_l_ready"], e + 1)
                for f in range(NF):
                    in_product(e, "g", f)
                    if f:
                        turn_hidden(e, f - 1)
                    in_product(e, "u", f)
                    if f:
                        down_product(e, f - 1, e)

            expert(0, first=True)
            with pe.Fori(1, E) as e:
                expert(e)
            turn_hidden(E - 1, 3)
            down_product(E - 1, 3, E)


def build(nc, **arrays):
    with ExitStack() as stack:
        program(nc, stack, **arrays)


_INS = ['x', 'c', 'ctx', 'c_ctx', 'ada_w', 'ada_b', 'norm_mix_g', 'norm_ffn_g', 'final_g', 'a_w_in', 'a_conv_w',
        'a_conv_b', 'a_gate_wa', 'a_gate_ba', 'a_gate_wx', 'a_gate_bx', 'a_lambda', 'a_w_out', 'router_w',
        'exp_w_gate', 'exp_w_up', 'exp_w_down']


def kernel(**inputs):
    import numpy as _np
    import concourse.bacc as _bacc
    from concourse import mybir as _mybir
    from concourse.bass_utils import run_bass_kernel_spmd as _run

    nc = _bacc.Bacc("TRN2", target_bir_lowering=False, num_devices=1)
    arrays, args = {}, {}
    for name in _INS:
        a = _np.ascontiguousarray(inputs[name])
        arrays[f"in_{name}_dram"] = a
        args[name] = nc.dram_tensor(f"in_{name}_dram", a.shape, _mybir.dt.from_np(a.dtype), kind="ExternalInput").ap()
    out = nc.dram_tensor("out_0_dram", inputs["x"].shape, _mybir.dt.float32, kind="ExternalOutput").ap()
    build(nc, out=out, **args)
    r = _run(nc, [arrays], core_ids=[0])
    return r.results[0]["out_0_dram"]
```
